# Optimizing a Trainium2 kernel written in Bass

```python
import math
import jax, jax.numpy as jnp
from jax import lax
import numpy as np

D_MODEL = 1024
BATCH = 1
SEQ = 1024
DEPTH = 1

CTX_LEN = 256
GRID_W = 64
CHUNK = 64
NORM_EPS = 1e-6
GDN_HEADS = 4
GDN_DK = 128
GDN_DV = 128
GDN_QKV = 3 * GDN_HEADS * GDN_DK
GLA_HEADS = 4
GLA_DK = 64
GLA_DV = 128
GLA_RANK = 16
GLA_NORMALIZER = 16.0
D_FF = 2816
SPLITS = (GDN_HEADS * GDN_DK, GDN_HEADS * GDN_DK, GDN_HEADS * GDN_DV, GDN_HEADS * GDN_DV,
          2 * GDN_HEADS, 2 * GDN_HEADS,
          GLA_HEADS * GLA_DK, GLA_HEADS * GLA_DK, GLA_HEADS * GLA_DV, GLA_HEADS * GLA_DV, 2 * GLA_RANK)
D_IN_PROJ = sum(SPLITS)
MIX_WIDTH = GDN_HEADS * GDN_DV + GLA_HEADS * GLA_DV

kernel_name = "hybrid_gdn_gla_prefix_dit"

def _rms_norm(x, gain):
    xf = x.astype(jnp.float32)
    y = xf * lax.rsqrt(jnp.mean(xf * xf, axis=-1, keepdims=True) + NORM_EPS)
    return (y * gain).astype(x.dtype)

def _modulate(h, shift, scale):
    return h * (1.0 + scale) + shift

def _heads(t, n_heads):
    b, l, cdim = t.shape
    return t.reshape(b, l, n_heads, cdim // n_heads).transpose(0, 2, 1, 3)

def _merge_heads(t):
    b, h, l, d = t.shape
    return t.transpose(0, 2, 1, 3).reshape(b, l, h * d)

def _l2norm(t):
    return t * lax.rsqrt(jnp.sum(t * t, axis=-1, keepdims=True) + 1e-6)

def _flip(t):
    return jnp.flip(t, axis=2)

def _conv1d_centred(x, w):
    l = x.shape[1]
    xp = jnp.pad(x, ((0, 0), (1, 1), (0, 0)))
    return xp[:, :l] * w[0] + xp[:, 1:l + 1] * w[1] + xp[:, 2:] * w[2]

def _conv_grid_3x3(x, w, b):
    bsz, l, cdim = x.shape
    rows = l // GRID_W
    img = x.reshape(bsz, rows, GRID_W, cdim)
    out = lax.conv_general_dilated(img, w[:, :, None, :], window_strides=(1, 1), padding="SAME",
                                   dimension_numbers=("NHWC", "HWIO", "NHWC"), feature_group_count=cdim)
    return out.reshape(bsz, l, cdim) + b

def _to_chunks(t):
    b, h, l = t.shape[:3]
    t = t.reshape(b, h, l // CHUNK, CHUNK, *t.shape[3:])
    return jnp.moveaxis(t, 2, 0)

def _from_chunks(t):
    t = jnp.moveaxis(t, 0, 2)
    b, h, n, cs, d = t.shape
    return t.reshape(b, h, n * cs, d)

def _gdn_scan(q, k, v, g, beta, s0):
    q, k, v, g, beta = map(_to_chunks, (q, k, v, g, beta))
    dv = v.shape[-1]
    gc = jnp.cumsum(g, axis=-1)
    incl = jnp.tril(jnp.ones((CHUNK, CHUNK), dtype=bool))
    strict = jnp.tril(jnp.ones((CHUNK, CHUNK), dtype=bool), -1)
    diff = gc[..., :, None] - gc[..., None, :]
    decay = jnp.where(incl, jnp.exp(jnp.where(incl, diff, 0.0)), 0.0)
    kb = k * beta[..., None]
    lower = jnp.where(strict, jnp.einsum("nbhcd,nbhsd->nbhcs", kb, k) * decay, 0.0)
    rhs = jnp.concatenate([v * beta[..., None], kb * jnp.exp(gc)[..., None]], axis=-1)
    sol = lax.linalg.triangular_solve(jnp.eye(CHUNK, dtype=lower.dtype) + lower, rhs,
                                      left_side=True, lower=True, unit_diagonal=True)
    u, w = sol[..., :dv], sol[..., dv:]
    attn = jnp.einsum("nbhcd,nbhsd->nbhcs", q, k) * decay

    def step(S, xs):
        q_c, k_c, u_c, w_c, a_c, g_c = xs
        v_new = u_c - jnp.einsum("bhcd,bhde->bhce", w_c, S)
        o = (jnp.einsum("bhcd,bhde->bhce", q_c * jnp.exp(g_c)[..., None], S)
             + jnp.einsum("bhcs,bhse->bhce", a_c, v_new))
        g_last = g_c[..., -1:]
        S = S * jnp.exp(g_last)[..., None] + jnp.einsum(
            "bhcd,bhce->bhde", k_c * jnp.exp(g_last - g_c)[..., None], v_new)
        return S, o

    s_final, o = lax.scan(step, s0, (q, k, u, w, attn, gc))
    return _from_chunks(o), s_final

def _gla_scan(q, k, v, gk, s0):
    q, k, v, gk = map(_to_chunks, (q, k, v, gk))
    gc = jnp.cumsum(gk, axis=-2)
    incl = jnp.tril(jnp.ones((CHUNK, CHUNK), dtype=bool))[:, :, None]

    def step(S, xs):
        q_c, k_c, v_c, g_c = xs
        o_inter = jnp.einsum("bhcd,bhde->bhce", q_c * jnp.exp(g_c), S)
        diff = g_c[..., :, None, :] - g_c[..., None, :, :]
        dec = jnp.where(incl, jnp.exp(jnp.where(incl, diff, 0.0)), 0.0)
        attn = jnp.einsum("bhcd,bhsd,bhcsd->bhcs", q_c, k_c, dec)
        o = o_inter + jnp.einsum("bhcs,bhse->bhce", attn, v_c)
        g_last = g_c[..., -1:, :]
        S = S * jnp.exp(g_last)[..., 0, :, None] + jnp.einsum(
            "bhcd,bhce->bhde", k_c * jnp.exp(g_last - g_c), v_c)
        return S, o

    s_final, o = lax.scan(step, s0, (q, k, v, gc))
    return _from_chunks(o), s_final

def _bidirectional(scan_fn, lat_f, lat_b, ctx_f, ctx_b, s0):
    o_cf, s_cf = scan_fn(*ctx_f, s0)
    o_cb, s_cb = scan_fn(*[_flip(t) for t in ctx_b], s0)
    o_lf, _ = scan_fn(*lat_f, s_cf)
    o_lb, _ = scan_fn(*[_flip(t) for t in lat_b], s_cb)
    return o_lf + _flip(o_lb), o_cf + _flip(o_cb)

def _gdn_prepare(q, k, v, a, b, conv_w, a_log, dt_bias):
    qkv = jax.nn.silu(_conv1d_centred(jnp.concatenate([q, k, v], axis=-1), conv_w))
    q, k, v = jnp.split(qkv, 3, axis=-1)
    q = _l2norm(_heads(q, GDN_HEADS)) * (GDN_DK ** -0.5)
    k = _l2norm(_heads(k, GDN_HEADS))
    v = _heads(v, GDN_HEADS)
    bsz, l = a.shape[:2]
    a = a.reshape(bsz, l, 2, GDN_HEADS)
    g = -jnp.exp(a_log) * jax.nn.softplus(a + dt_bias)
    beta = jax.nn.sigmoid(b.reshape(bsz, l, 2, GDN_HEADS))
    return q, k, v, g.transpose(2, 0, 3, 1), beta.transpose(2, 0, 3, 1)

def _gla_prepare(q, k, v, lr, w_gk, b_gk):
    q = _heads(q, GLA_HEADS) * (GLA_DK ** -0.5)
    k = _heads(k, GLA_HEADS)
    v = _heads(v, GLA_HEADS)
    bsz, l = lr.shape[:2]
    lr = lr.reshape(bsz, l, 2, GLA_RANK)
    gk = jax.nn.log_sigmoid(jnp.einsum("blzr,zrc->zblc", lr, w_gk) + b_gk[:, None, None, :]) / GLA_NORMALIZER
    return q, k, v, _heads(gk[0], GLA_HEADS), _heads(gk[1], GLA_HEADS)

def _hybrid_mixer(h_lat, h_ctx, w_in, gdn_conv, gdn_a_log, gdn_dt_bias, gdn_norm,
                  gla_w_gk, gla_b_gk, gla_norm, w_out, with_ctx_out):
    idx = np.cumsum(SPLITS)[:-1].tolist()
    p_lat = jnp.split((h_lat @ w_in).astype(jnp.float32), idx, axis=-1)
    p_ctx = jnp.split((h_ctx @ w_in).astype(jnp.float32), idx, axis=-1)
    bsz = h_lat.shape[0]

    ql, kl, vl, gl, bl = _gdn_prepare(p_lat[0], p_lat[1], p_lat[2], p_lat[4], p_lat[5], gdn_conv, gdn_a_log, gdn_dt_bias)
    qc, kc, vc, gcx, bc = _gdn_prepare(p_ctx[0], p_ctx[1], p_ctx[2], p_ctx[4], p_ctx[5], gdn_conv, gdn_a_log, gdn_dt_bias)
    s0_a = jnp.zeros((bsz, GDN_HEADS, GDN_DK, GDN_DV), jnp.float32)
    o_a_lat, o_a_ctx = _bidirectional(
        _gdn_scan,
        (ql, kl, vl, gl[0], bl[0]), (ql, kl, vl, gl[1], bl[1]),
        (qc, kc, vc, gcx[0], bc[0]), (qc, kc, vc, gcx[1], bc[1]), s0_a)

    lq, lk, lv, lgf, lgb = _gla_prepare(p_lat[6], p_lat[7], p_lat[8], p_lat[10], gla_w_gk, gla_b_gk)
    cq, ck, cv, cgf, cgb = _gla_prepare(p_ctx[6], p_ctx[7], p_ctx[8], p_ctx[10], gla_w_gk, gla_b_gk)
    s0_b = jnp.zeros((bsz, GLA_HEADS, GLA_DK, GLA_DV), jnp.float32)
    o_b_lat, o_b_ctx = _bidirectional(
        _gla_scan,
        (lq, lk, lv, lgf), (lq, lk, lv, lgb),
        (cq, ck, cv, cgf), (cq, ck, cv, cgb), s0_b)

    def merge(o_a, z, o_b, gate, dtype):
        y_a = _merge_heads(_rms_norm(o_a, gdn_norm)) * jax.nn.silu(z)
        y_b = _merge_heads(_rms_norm(o_b, gla_norm)) * jax.nn.silu(gate)
        return (jnp.concatenate([y_a, y_b], axis=-1).astype(w_out.dtype) @ w_out).astype(dtype)

    y_lat = merge(o_a_lat, p_lat[3], o_b_lat, p_lat[9], h_lat.dtype)
    y_ctx = merge(o_a_ctx, p_ctx[3], o_b_ctx, p_ctx[9], h_ctx.dtype) if with_ctx_out else None
    return y_lat, y_ctx

def _conv_ffn(h, w_up, conv_w, conv_b, w_down, on_grid):
    u = h @ w_up
    u = _conv_grid_3x3(u, conv_w, conv_b) if on_grid else _conv1d_centred(u, conv_w[1]) + conv_b
    a, v = jnp.split(u, 2, axis=-1)
    return (jax.nn.silu(a) * v) @ w_down

def setup_inputs(seed: int = 0) -> dict:
    key = jax.random.key(seed)
    ks = jax.random.split(key, 24)
    n = jax.random.normal
    d = D_MODEL
    dt = jnp.exp(jax.random.uniform(ks[9], (DEPTH, 2, GDN_HEADS), minval=math.log(1e-3), maxval=math.log(0.1)))
    return {
        "x": n(ks[0], (BATCH, SEQ, d), jnp.float32),
        "c": n(ks[1], (BATCH, d), jnp.float32),
        "ctx": n(ks[2], (BATCH, CTX_LEN, d), jnp.float32),
        "c_ctx": n(ks[3], (d,), jnp.float32),
        "w_mod": n(ks[4], (DEPTH, d, 6 * d), jnp.float32) * d ** -0.5,
        "b_mod": n(ks[5], (DEPTH, 6 * d), jnp.float32) * 0.01,
        "norm1": 1.0 + 0.02 * n(ks[6], (DEPTH, d), jnp.float32),
        "w_in": n(ks[7], (DEPTH, d, D_IN_PROJ), jnp.float32) * d ** -0.5,
        "gdn_conv": n(ks[8], (DEPTH, 3, GDN_QKV), jnp.float32) * 3 ** -0.5,
        "gdn_a_log": jnp.log(jax.random.uniform(ks[10], (DEPTH, 2, GDN_HEADS), minval=1.0, maxval=16.0)),
        "gdn_dt_bias": dt + jnp.log(-jnp.expm1(-dt)),
        "gdn_norm": 1.0 + 0.02 * n(ks[11], (DEPTH, GDN_DV), jnp.float32),
        "gla_w_gk": n(ks[12], (DEPTH, 2, GLA_RANK, GLA_HEADS * GLA_DK), jnp.float32) * GLA_RANK ** -0.5,
        "gla_b_gk": 0.1 * n(ks[13], (DEPTH, 2, GLA_HEADS * GLA_DK), jnp.float32),
        "gla_norm": 1.0 + 0.02 * n(ks[14], (DEPTH, GLA_DV), jnp.float32),
        "w_out": n(ks[15], (DEPTH, MIX_WIDTH, d), jnp.float32) * MIX_WIDTH ** -0.5,
        "norm2": 1.0 + 0.02 * n(ks[16], (DEPTH, d), jnp.float32),
        "w_up": n(ks[17], (DEPTH, d, 2 * D_FF), jnp.float32) * d ** -0.5,
        "ffn_conv": n(ks[18], (DEPTH, 3, 3, 2 * D_FF), jnp.float32) / 3.0,
        "ffn_conv_b": 0.01 * n(ks[19], (DEPTH, 2 * D_FF), jnp.float32),
        "w_down": n(ks[20], (DEPTH, D_FF, d), jnp.float32) * D_FF ** -0.5,
        "final_norm": 1.0 + 0.02 * n(ks[21], (d,), jnp.float32),
    }

def reference(x, c, ctx, c_ctx, w_mod, b_mod, norm1, w_in, gdn_conv, gdn_a_log, gdn_dt_bias, gdn_norm,
              gla_w_gk, gla_b_gk, gla_norm, w_out, norm2, w_up, ffn_conv, ffn_conv_b, w_down, final_norm):
    sc_lat = jax.nn.silu(c)[:, None, :]
    sc_ctx = jax.nn.silu(c_ctx)
    for i in range(DEPTH):
        last = i == DEPTH - 1
        m_lat = jnp.split(sc_lat @ w_mod[i] + b_mod[i], 6, axis=-1)
        m_ctx = jnp.split(sc_ctx @ w_mod[i] + b_mod[i], 6, axis=-1)
        h_lat = _modulate(_rms_norm(x, norm1[i]), m_lat[0], m_lat[1])
        h_ctx = _modulate(_rms_norm(ctx, norm1[i]), m_ctx[0], m_ctx[1])
        y_lat, y_ctx = _hybrid_mixer(h_lat, h_ctx, w_in[i], gdn_conv[i], gdn_a_log[i], gdn_dt_bias[i], gdn_norm[i],
                                     gla_w_gk[i], gla_b_gk[i], gla_norm[i], w_out[i], not last)
        x = x + m_lat[2] * y_lat
        h_lat = _modulate(_rms_norm(x, norm2[i]), m_lat[3], m_lat[4])
        x = x + m_lat[5] * _conv_ffn(h_lat, w_up[i], ffn_conv[i], ffn_conv_b[i], w_down[i], True)
        if not last:
            ctx = ctx + m_ctx[2] * y_ctx
            h_ctx = _modulate(_rms_norm(ctx, norm2[i]), m_ctx[3], m_ctx[4])
            ctx = ctx + m_ctx[5] * _conv_ffn(h_ctx, w_up[i], ffn_conv[i], ffn_conv_b[i], w_down[i], False)
    return _rms_norm(x, final_norm)


_drawn_inputs = setup_inputs


def setup_inputs(seed=0):
    import zlib

    import numpy as np

    out = dict(_drawn_inputs(seed))
    spreads = {}
    factors = {'b_mod': 3.04,
     'norm1': 3.637,
     'gdn_norm': 22.363,
     'gla_b_gk': 2.762,
     'gla_norm': 25.128,
     'norm2': 14.099,
     'ffn_conv_b': 31.667,
     'final_norm': 7.215}
    for name, (base, spread) in spreads.items():
        noise = np.random.default_rng([zlib.crc32(name.encode()), seed]).standard_normal(out[name].shape)
        drawn = base * np.exp(spread * noise) if base else spread * noise
        out[name] = __import__('jax').numpy.asarray(drawn.astype(out[name].dtype))
    for name, factor in factors.items():
        out[name] = (out[name] * factor).astype(out[name].dtype)
    return out
```

```python
from contextlib import ExitStack

import concourse.bass as bass
from concourse import mybir

F32 = mybir.dt.float32
F32R = mybir.dt.float32r
U8 = mybir.dt.uint8
BF16 = mybir.dt.bfloat16
ACT = mybir.ActivationFunctionType
ALU = mybir.AluOpType
AX_X = mybir.AxisListType.X

P = 128
D = 1024
KT = D // P
LAT = 1024
CTX = 256
TOK = LAT + CTX
NL = LAT // P
NC = CTX // P
NT = NL + NC
H = 4
HW = H * P
GRID = 64
ROWS = LAT // GRID
FF = 2816
FT = FF // P
EPS = 1e-6
LEVELS = 7
CV = 1 + LAT + 1 + CTX + 1
CO = CV - 2
CTX_AT = LAT + 1

Q0, K0, V0, Z0, AB0 = 0, HW, 2 * HW, 3 * HW, 4 * HW
GQ0 = AB0 + 4 * H
GK0 = GQ0 + HW // 2
GV0 = GK0 + HW // 2
GG0 = GV0 + HW
LR0 = GG0 + HW
RANK = 16

BMOD, NORM1, NORM2, CONV, NGDN, NGLA, BGK, CLAT, CCTX, NPV = 0, 48, 56, 64, 100, 101, 102, 106, 114, 122
CTILES = 3 * H
NFC = 10 * 2 * FT // 4


def steps(eng, first, n, body, unroll=2):
    if n <= unroll:
        for u in range(n):
            body(first + u, u)
    else:
        with eng.Fori(0, n // unroll) as i:
            for u in range(unroll):
                body(i * unroll + (first + u), u)


def at(start, size):
    return bass.ds(start, size)


def bc(ap, n):
    return ap.unsqueeze(2).to_broadcast([ap.shape[0], ap.shape[1], n])


def heads(ap):
    return ap.rearrange("p (h n) -> p h n", h=H)


def half(ap, m, side):
    return ap.rearrange("p (b h x) -> p b h x", h=2, x=m)[:, :, side, :]


def program(nc, x, c, ctx, c_ctx, w_mod, b_mod, norm1, w_in, gdn_conv, gdn_a_log, gdn_dt_bias, gdn_norm,
            gla_w_gk, gla_b_gk, gla_norm, w_out, norm2, w_up, ffn_conv, ffn_conv_b, w_down, final_norm, out,
            stop=99):
    BASE = 16512

    def place(name, shape, kb, dt=F32):
        return nc.alloc_sbuf_tensor_at(name, shape, dt, offset=BASE + int(kb * 1024))

    es = ExitStack()
    with es:
        sems = []

        def sem(name):
            sems.append(nc.alloc_semaphore(name))
            return sems[-1]

        def recycle():
            nc.clear_and_free_semaphores(sems)
            sems.clear()
            nc.all_engine_barrier()

        PS = es.enter_context(nc.psum_tensor("PS", [P, 8, 512], F32))

        small_end = [BASE + 5888]

        def small(name, shape):
            size = 4
            for n in shape[1:]:
                size *= n
            t = nc.alloc_sbuf_tensor_at(name, shape, F32, offset=small_end[0])
            small_end[0] += -(-size // 32) * 32
            assert small_end[0] <= BASE + 15 * 1024
            return t

        ident = place("ident", [P, P], 0)
        ones = place("ones", [P, P], 0.5)
        tri = place("tri", [P, 2, P], 1)
        suf = place("suf", [P, 2, P], 2)
        quad = place("quad", [P, 2, LEVELS, P], 3, U8)
        both = place("both", [P, LEVELS + 1, P], 4.75, U8)
        vcol = small("vcol", [P, P])
        fcol = small("fcol", [P, 4 * NFC])
        mods = small("mods", [P, 48, 2])
        gain = small("gain", [P, 3 * KT])
        scol = small("scol", [P, KT, 2])
        epsc = small("epsc", [P, 1])
        ab = small("ab", [P, NT, 16])
        gdec = small("gdec", [P, NT, 8])
        beta = small("beta", [P, NT, 8])
        nbeta = small("nbeta", [P, NT, 8])
        gsum = small("gsum", [P, 2, 2, NT * H])
        gexp = small("gexp", [P, 2, 2, NT * H])
        nbe = small("nbe", [P, 2, NT * H])
        hbias = small("hbias", [P, 2, 8])
        gtmp = small("gtmp", [P, 2, NT, 8])
        wgk = small("wgk", [32, 2, 256])

        hT = place("hT", [P, KT, TOK], 15)

        wm = [place(f"wm{i}", [P, KT, 512], 55 + 16 * i) for i in range(4)]
        xt = place("xt", [P, NT, D], 119)
        sq0 = place("sq0", [P, 2, D], 159)
        ssq = place("ssq", [P, NT], 167)
        rms = place("rms", [P, NT], 167.125)
        rstd = place("rstd", [P, NT], 167.25)
        mtmp = place("mtmp", [P, 2 * LEVELS, P], 168)
        vrow = place("vrow", [P, P], 176)
        frow = place("frow", [P, 4, P], 177)
        mrow = place("mrow", [2, 12, 512], 179)

        s_vec = sem("small_vectors_in")
        s_fv = sem("ffn_vectors_in")
        s_hb = sem("head_biases_in")
        s_wgk = sem("wgk_in")
        s_cst = sem("constants")
        s_pool = sem("pool_step")
        s_vt = sem("vectors_turned")
        s_vc = sem("vector_columns")
        s_sc = sem("silu_c")
        s_wm = [sem(f"w_mod_in{i}") for i in range(4)]
        s_wmu = sem("w_mod_used")
        s_mod = sem("modulation_ready")
        s_mr = sem("modulation_row")
        s_mt = sem("modulation_turned")
        s_gain = sem("gains_ready")
        s_xin = sem("x_in")
        s_xs = sem("x_squares")
        s_xr = sem("x_rms")
        s_xi = sem("x_rstd")
        s_xn = sem("x_normed")
        s_xt = sem("x_turned")
        s_hta = sem("h_by_act")
        s_htv = sem("h_by_dve")
        s_wz = sem("wgk_zeroed")

        wmv = w_mod[0].rearrange("(k p) n -> p k n", p=P)
        x_tok, ctx_tok = x[0], ctx[0]

        with nc.Block() as block:
            @block.sync
            def _(sp):
                for row, n, src in ((BMOD, 48, b_mod[0]), (NORM1, 8, norm1[0]), (NORM2, 8, norm2[0]),
                                    (NGDN, 1, gdn_norm[0]), (NGLA, 1, gla_norm[0]), (CLAT, 8, c[0]), (CCTX, 8, c_ctx)):
                    sp.dma_start(vrow[row:row + n, :], src.rearrange("(a n) -> a n", n=P)).then_inc(s_vec, 16)
                sp.dma_start(vrow[CONV:CONV + 3 * CTILES, :], gdn_conv[0].rearrange("k (a n) -> (k a) n", n=P)).then_inc(s_vec, 16)
                sp.dma_start(vrow[BGK:BGK + 4, :], gla_b_gk[0].rearrange("k (a n) -> (k a) n", n=P)).then_inc(s_vec, 16)
                with sp.Fori(0, 3) as i:
                    for v in range(4):
                        sp.wait_ge(s_wmu, i * 4 + (v + 1))
                        sp.dma_start(wm[v][:, :, :], wmv[:, :, at(i * 2048 + v * 512, 512)]).then_inc(s_wm[v], 16)

            @block.gpsimd
            def _(g):
                g.sem_inc(s_wmu, 4)
                g.memset(ident[:, :], 0.0).then_inc(s_pool, 1)
                g.memset(ones[:, :], 1.0).then_inc(s_pool, 1)
                g.memset(mtmp[:, :, :], 0.0).then_inc(s_pool, 1)
                g.memset(epsc[:, :], EPS).then_inc(s_pool, 1)
                g.memset(wgk[:, :, :], 0.0).then_inc(s_wz, 1)
                fr = ffn_conv[0].rearrange("a b (t n) -> (a b t) n", n=P)
                fb = ffn_conv_b[0].rearrange("(t n) -> t n", n=P)
                g.wait_ge(s_pool, 4)
                g.affine_select(out=ident[:, :], in_=ident[:, :], compare_op=ALU.not_equal, fill=1.0, base=0,
                                pattern=[[-1, P]], channel_multiplier=1).then_inc(s_cst, 1)
                for dst, base, step in ((tri[:, 0, :], 0, 1), (tri[:, 1, :], 0, -1), (suf[:, 0, :], -1, -1), (suf[:, 1, :], -1, 1)):
                    g.affine_select(out=dst, in_=ones[:, :], compare_op=ALU.is_ge, fill=0.0, base=base,
                                    pattern=[[step, P]], channel_multiplier=-step).then_inc(s_cst, 1)
                n = 4
                for lvl in range(LEVELS):
                    m = 1 << lvl
                    for side in range(2):
                        v = mtmp[:, side * LEVELS + lvl, :].rearrange("p (b h x) -> p b h x", h=2, x=m)[:, :, side, :]
                        lo = m if side == 0 else 0
                        src = ones[:, 0:64].rearrange("p (b x) -> p b x", x=m)
                        g.affine_select(out=v, in_=src, compare_op=ALU.is_ge, fill=0.0, base=-lo,
                                        pattern=[[-2 * m, 64 // m], [0, m]], channel_multiplier=1).then_inc(s_pool, 1)
                        n += 1
                        g.wait_ge(s_pool, n)
                        g.affine_select(out=v, in_=v, compare_op=ALU.is_ge, fill=0.0, base=lo + m - 1,
                                        pattern=[[2 * m, 64 // m], [0, m]], channel_multiplier=-1).then_inc(s_cst, 1)
                g.wait_ge(s_wz, 1)
                g.dma_start(wgk[0:RANK, 0, :], gla_w_gk[0, 0]).then_inc(s_wgk, 16)
                g.dma_start(wgk[RANK:2 * RANK, 1, :], gla_w_gk[0, 1]).then_inc(s_wgk, 16)
                for j in range(4):
                    lo, hi = j * NFC, min((j + 1) * NFC, 18 * FT)
                    g.dma_start(frow[0:hi - lo, j, :], fr[lo:hi, :]).then_inc(s_fv, 16)
                g.dma_start(frow[NFC - 2 * FT:NFC, 3, :], fb).then_inc(s_fv, 16)
                g.dma_start(hbias[:, 0, :], gdn_dt_bias.rearrange("o a b -> o (a b)").to_broadcast([P, 8])).then_inc(s_hb, 16)
                g.dma_start(hbias[:, 1, :], gdn_a_log.rearrange("o a b -> o (a b)").to_broadcast([P, 8])).then_inc(s_hb, 16)

            @block.tensor
            def _(pe):
                pe.wait_ge(s_cst, 1)
                pe.wait_ge(s_vec, 9 * 16)
                pe.transpose(PS[:, 1, 0:NPV], vrow[0:NPV, :], ident[0:NPV, 0:NPV]).then_inc(s_vt, 1)
                pe.wait_ge(s_sc, 2)

                def modmm(i, v):
                    pe.wait_ge(s_wm[v], (i + 1) * 16)
                    for k in range(KT):
                        mm = pe.matmul(PS[0:2, 3 + v % 2, :], scol[:, k, :], wm[v][:, k, :], start=(k == 0), stop=(k == KT - 1))
                    mm.then_inc(s_wmu, 1)

                with pe.Fori(0, 3) as i:
                    for v in range(4):
                        pe.wait_ge(s_mr, i * 4 + (v + 1))
                        modmm(i, v)
                pe.wait_ge(s_mr, 12 + 2)
                for j in range(48):
                    tr = pe.transpose(PS[:, 0, 2 * j:2 * j + 2], mrow[0:2, j // 4, (j % 4) * P:(j % 4 + 1) * P], ident[0:2, 0:2])
                tr.then_inc(s_mt, 1)
                pe.wait_ge(s_fv, 5 * 16)
                for j in range(4):
                    tr = pe.transpose(PS[:, 1, P + 0:P + NFC] if j == 0 else PS[:, 2, (j - 1) * P:(j - 1) * P + NFC],
                                      frow[0:NFC, j, :], ident[0:NFC, 0:NFC])
                tr.then_inc(s_vt, 1)

                def turn(t, u):
                    pe.wait_ge(s_xn, t + 1)
                    pe.wait_ge(s_hta, t + 1)
                    pe.wait_ge(s_htv, t + 1)
                    for k in range(KT):
                        tr = pe.transpose(PS[:, 4 + 2 * u + k // 4, (k % 4) * P:(k % 4 + 1) * P],
                                          xt[:, t, k * P:(k + 1) * P], ident[:, :])
                    tr.then_inc(s_xt, 1)
                for t in range(NT):
                    turn(t, t % 2)

            @block.scalar
            def _(a):
                for q in range(2):
                    a.dma_start(xt[:, q * 4:q * 4 + 4, :], x_tok.rearrange("(t p) n -> p t n", p=P)[:, q * 4:q * 4 + 4, :]).then_inc(s_xin, 16)
                a.dma_start(xt[:, NL:NT, :], ctx_tok.rearrange("(t p) n -> p t n", p=P)).then_inc(s_xin, 16)
                a.sem_inc(s_hta, 2)
                a.wait_ge(s_vc, 1)
                a.activation(scol[:, :, 0], vcol[:, CLAT:CLAT + KT], ACT.Silu).then_inc(s_sc, 1)
                a.activation(scol[:, :, 1], vcol[:, CCTX:CCTX + KT], ACT.Silu).then_inc(s_sc, 1)

                a.wait_ge(s_xin, 48)
                for t in range(NT):
                    if t >= 2:
                        a.wait_ge(s_xs, t - 1)
                    a.activation(sq0[:, t % 2, :], xt[:, t, :], ACT.Square, accum_out=ssq[:, t:t + 1]).then_inc(s_xs, 1)
                a.wait_ge(s_xs, NT)
                a.activation(rms[:, :], ssq[:, :], ACT.Sqrt, scale=1.0 / D, bias=epsc[:, :]).then_inc(s_xr, 1)

                def evac(t, u, row, half):
                    a.wait_ge(s_xt, t + 1)
                    for k in range(4):
                        ev = a.activation(hT[:, k, at(t * P, P)], PS[:, 4 + 2 * u, k * P:(k + 1) * P], ACT.Identity,
                                          scale=gain[:, row * KT + k:row * KT + k + 1], bias=mods[:, k, half:half + 1])
                    ev.then_inc(s_hta, 1)
                a.wait_ge(s_gain, 1)
                steps(a, 0, NL, lambda t, u: evac(t, u, 0, 0))
                steps(a, NL, NC, lambda t, u: evac(t, u, 1, 1))

            @block.vector
            def _(v):
                v.sem_inc(s_htv, 2)
                v.wait_ge(s_vt, 1)
                v.tensor_copy(vcol[:, 0:NPV], PS[:, 1, 0:NPV]).then_inc(s_vc, 1)
                v.wait_ge(s_cst, 1 + 4 + 2 * LEVELS)
                v.tensor_copy(quad[:, :, :, :].rearrange("p a l n -> p (a l) n"), mtmp[:, :, :])
                v.tensor_tensor(both[:, 0:LEVELS, :], mtmp[:, 0:LEVELS, :], mtmp[:, LEVELS:2 * LEVELS, :], ALU.add)
                v.tensor_copy(both[:, LEVELS, :], ident[:, :])

                v.wait_ge(s_xr, 1)
                v.reciprocal(rstd[:, :], rms[:, :]).then_inc(s_xi, 1)
                v.wait_ge(s_xi, 1)
                for t in range(NT):
                    v.tensor_scalar(xt[:, t, :], xt[:, t, :], rstd[:, t:t + 1], None, ALU.mult).then_inc(s_xn, 1)

                def evac(t, u, row, half):
                    v.wait_ge(s_xt, t + 1)
                    for k in range(4, KT):
                        ev = v.tensor_scalar(hT[:, k, at(t * P, P)], PS[:, 5 + 2 * u, (k - 4) * P:(k - 3) * P],
                                             gain[:, row * KT + k:row * KT + k + 1], mods[:, k, half:half + 1],
                                             ALU.mult, ALU.add)
                    ev.then_inc(s_htv, 1)
                v.sem_inc(s_mr, 2)

                def row(p, u):
                    v.wait_ge(s_wmu, p + 5)
                    v.tensor_copy(mrow[:, at(p, 1), :].rearrange("p a n -> p (a n)"), PS[0:2, 3 + u, :]).then_inc(s_mr, 1)
                steps(v, 0, 12, row)
                v.wait_ge(s_mt, 1)
                v.tensor_tensor(mods[:, :, :], PS[:, 0, 0:96].rearrange("p (a b) -> p a b", b=2),
                                bc(vcol[:, BMOD:BMOD + 48], 2), ALU.add).then_inc(s_mod, 1)
                v.wait_ge(s_mod, 1)
                for row, sc_at, half, nrm in ((0, KT, 0, NORM1), (1, KT, 1, NORM1), (2, 4 * KT, 0, NORM2)):
                    gm = v.scalar_tensor_tensor(out=gain[:, row * KT:(row + 1) * KT], in0=mods[:, sc_at:sc_at + KT, half],
                                                scalar=1.0, in1=vcol[:, nrm:nrm + KT], op0=ALU.add, op1=ALU.mult)
                gm.then_inc(s_gain, 1)
                v.wait_ge(s_vt, 2)
                v.tensor_copy(fcol[:, 0:NFC], PS[:, 1, P:P + NFC])
                v.tensor_copy(fcol[:, NFC:4 * NFC].rearrange("p (a n) -> p a n", a=3),
                              PS[:, 2, 0:3 * P].rearrange("p (a n) -> p a n", a=3)[:, :, 0:NFC]).then_inc(s_gain, 1)
                v.wait_ge(s_gain, 2)

                steps(v, 0, NL, lambda t, u: evac(t, u, 0, 0))
                steps(v, NL, NC, lambda t, u: evac(t, u, 1, 1))

        if stop == 0:
            return


        wq = [place(f"wq{i}", [P, KT, P], 55 + 4 * i) for i in range(3)]
        raw = [place(f"raw{i}", [P, CV], 67 + 5.0625 * i) for i in range(3)]
        qT = place("qT", [P, H, LAT], 86)
        kT = place("kT", [P, H, CO], 102)
        vtok = place("vtok", [P, NT, HW], 122.25)
        cv = [place(f"cv{i}", [P, CO], 143 + 5.0625 * i) for i in range(3)]
        csq = place("csq", [P, CO], 159)
        crn = place("crn", [P, CO], 164.5)
        lrab = place("lrab", [48, TOK], 192)

        s_pad = sem("pads_zero")
        s_win = [sem(f"w_qkv_in{i}") for i in range(3)]
        s_mm = [sem(f"qkv_products{i}") for i in range(3)]
        s_bank = [sem(f"qkv_banks_free{i}") for i in range(3)]
        s_raw = [sem(f"qkv_raw{i}") for i in range(3)]
        s_cs = [sem(f"conv_step{i}") for i in range(3)]
        s_sil = [sem(f"qkv_silu{i}") for i in range(3)]
        s_csq = [sem(f"qk_squares{i}") for i in range(2)]
        s_css = [sem(f"qk_square_sums{i}") for i in range(2)]
        s_qu = sem("q_unit_norm_used")
        s_cri = [sem(f"qk_inverse_norms{i}") for i in range(2)]
        s_vtt = sem("v_turned")
        s_lw = sem("w_lrab_in")
        s_lm = sem("lrab_product")
        s_la = sem("lrab_copied")
        s_lt = sem("lrab_turned")
        s_gd = sem("gate_by_dve")
        s_ga = sem("gate_by_act")
        s_gm = sem("gate_sums")
        s_gdone = sem("gates_ready")

        win = w_in[0].rearrange("(k p) n -> p k n", p=P)
        BANK = (0, 2, 5)
        PARTS = (((0, 512), (512, 512)),) + (((0, 512), (512, 512), (1024, 256)),) * 2

        def tap(j, kind, h):
            r = CONV + j * CTILES + kind * H
            return vcol[:, at(r + h, 1)]

        with nc.Block() as block:
            @block.sync
            def _(sp):
                def load(h):
                    for kind in range(3):
                        if not isinstance(h, int):
                            sp.wait_ge(s_mm[kind], h)
                        sp.dma_start(wq[kind][:, :, :], win[:, :, at(h * P + kind * HW, P)]).then_inc(s_win[kind], 16)
                load(0)
                with sp.Fori(1, H) as h:
                    load(h)
                sp.wait_ge(s_mm[0], H)
                sp.dma_start(wq[0][:, :, 0:2 * RANK], win[:, :, LR0:LR0 + 2 * RANK]).then_inc(s_lw, 16)
                sp.dma_start(wq[0][:, :, 2 * RANK:48], win[:, :, AB0:AB0 + 16]).then_inc(s_lw, 16)

            @block.tensor
            def _(pe):
                def product(kind, h):
                    pe.wait_ge(s_win[kind], h * 16 + 16)
                    pe.wait_ge(s_bank[kind], h + 1)
                    for b, (t0, n) in enumerate(PARTS[kind]):
                        for k in range(KT):
                            mm = pe.matmul(PS[:, BANK[kind] + b, 0:n], wq[kind][:, k, :], hT[:, k, t0:t0 + n],
                                           start=(k == 0), stop=(k == KT - 1))
                    mm.then_inc(s_mm[kind], 1)

                def sums(kind, h):
                    pe.wait_ge(s_csq[kind], h + 1)
                    for b, (t0, n) in enumerate(PARTS[kind]):
                        c0 = t0 + (t0 == LAT)
                        mm = pe.matmul(PS[:, BANK[kind] + b, 0:n], ones[:, :], csq[:, c0:c0 + n], start=True, stop=True)
                    mm.then_inc(s_css[kind], 1)

                def turn_v(h):
                    pe.wait_ge(s_sil[2], h + 1)
                    for ch in range(NT):
                        c0 = ch * P + (ch >= NL)
                        tr = pe.transpose(PS[:, 5 + ch // 4, (ch % 4) * P:(ch % 4 + 1) * P], cv[2][:, c0:c0 + P], ident[:, :])
                    tr.then_inc(s_vtt, 1)

                def head(h, last_v):
                    product(0, h)
                    if last_v is not None:
                        turn_v(last_v)
                    product(1, h)
                    sums(0, h)
                    product(2, h)
                    sums(1, h)
                head(0, None)
                with pe.Fori(1, H) as h:
                    head(h, h - 1)
                pe.wait_ge(s_lw, 32)
                pe.wait_ge(s_bank[0], H + 1)
                pe.wait_ge(s_bank[1], H + 1)
                for b, (t0, n) in enumerate(PARTS[1]):
                    for k in range(KT):
                        mm = pe.matmul(PS[0:48, b, 0:n], wq[0][:, k, 0:48], hT[:, k, t0:t0 + n],
                                       start=(k == 0), stop=(k == KT - 1))
                mm.then_inc(s_lm, 1)
                turn_v(H - 1)
                pe.wait_ge(s_la, 1)
                for ch in range(NT):
                    tr = pe.transpose(PS[:, 3, ch * 48:(ch + 1) * 48], lrab[:, ch * P:(ch + 1) * P], ident[0:48, 0:48])
                tr.then_inc(s_lt, 1)
                pe.wait_ge(s_gd, 3)
                for kind, m in ((0, tri), (1, suf)):
                    for d in range(2):
                        mm = pe.matmul(PS[:, 4, (2 * kind + d) * 40:(2 * kind + d + 1) * 40].rearrange("p (c h) -> p c h", h=H),
                                       m[:, d, :], gdec[:, :, 4 * d:4 * d + 4], start=True, stop=True)
                mm.then_inc(s_gm, 1)

            @block.scalar
            def _(a):
                a.sem_inc(s_bank[0], 1)
                a.sem_inc(s_bank[1], 1)

                def evac(kind, h):
                    a.wait_ge(s_mm[kind], h + 1)
                    if kind == 2:
                        a.wait_ge(s_pad, 1)
                    b = BANK[kind]
                    ev = a.activation(raw[kind][:, 1:1 + LAT], PS[:, b:b + 2, :].rearrange("p a n -> p (a n)"), ACT.Copy)
                    if kind:
                        ev = a.activation(raw[kind][:, 2 + LAT:2 + LAT + CTX], PS[:, b + 2, 0:CTX], ACT.Copy)
                    ev.then_inc(s_raw[kind], 1)

                def silu(kind, h):
                    n = CO if kind else LAT
                    a.wait_ge(s_cs[kind], h * 3 + 3)
                    a.activation(cv[kind][:, 0:n], cv[kind][:, 0:n], ACT.Silu).then_inc(s_sil[kind], 1)
                    if kind < 2:
                        a.wait_ge(s_sil[kind], h + 1)
                        a.activation(csq[:, 0:n], cv[kind][:, 0:n], ACT.Square).then_inc(s_csq[kind], 1)

                def root(kind, h):
                    a.wait_ge(s_css[kind], h + 1)
                    if kind:
                        a.wait_ge(s_qu, h + 1)
                    b = BANK[kind]
                    ev = a.activation(crn[:, 0:LAT], PS[:, b:b + 2, :].rearrange("p a n -> p (a n)"), ACT.Sqrt, bias=epsc[:, :])
                    if kind:
                        ev = a.activation(crn[:, CTX_AT:CO], PS[:, b + 2, 0:CTX], ACT.Sqrt, bias=epsc[:, :])
                        ev.then_inc(s_bank[kind], 1)
                    else:
                        ev.then_inc(s_bank[kind], 1)

                def head(h, u):
                    evac(0, h)
                    silu(0, h)
                    evac(1, h)
                    root(0, h)
                    silu(1, h)
                    evac(2, h)
                    root(1, h)
                    silu(2, h)
                steps(a, 0, H, head, 1)
                a.wait_ge(s_lm, 1)
                for b, (t0, n) in enumerate(PARTS[1]):
                    ev = a.activation(lrab[:, t0:t0 + n], PS[0:48, b, 0:n], ACT.Copy)
                ev.then_inc(s_la, 1)
                a.wait_ge(s_gd, 2)
                a.activation(gtmp[:, 1, :, :], gtmp[:, 0, :, :], ACT.Abs).then_inc(s_ga, 1)
                a.activation(hbias[:, 1, :], hbias[:, 1, :], ACT.Exp).then_inc(s_ga, 1)
                a.wait_ge(s_ga, 2)
                a.activation(gtmp[:, 1, :, :], gtmp[:, 1, :, :], ACT.Exp, scale=-1.0).then_inc(s_ga, 1)
                a.wait_ge(s_ga, 3)
                a.activation(gtmp[:, 1, :, :], gtmp[:, 1, :, :], ACT.Ln, bias=1.0).then_inc(s_ga, 1)
                a.activation(beta[:, :, :], ab[:, :, 8:16], ACT.Sigmoid).then_inc(s_ga, 1)
                a.wait_ge(s_gd, 4)
                a.activation(gexp[:, :, :, :], gsum[:, :, :, :], ACT.Exp).then_inc(s_ga, 1)

            @block.vector
            def _(v):
                v.sem_inc(s_bank[2], 1)
                for kind in range(3):
                    v.memset(raw[kind][:, 0:1], 0.0)
                    v.memset(raw[kind][:, 1 + LAT:2 + LAT], 0.0)
                    z = v.memset(raw[kind][:, CV - 1:CV], 0.0)
                z.then_inc(s_pad, 1)
                v.wait_ge(s_pad, 1)

                def conv(kind, h):
                    n = CO if kind else LAT
                    v.wait_ge(s_raw[kind], h + 1)
                    v.tensor_scalar(cv[kind][:, 0:n], raw[kind][:, 1:1 + n], tap(1, kind, h), None, ALU.mult).then_inc(s_cs[kind], 1)
                    for j in (0, 2):
                        v.wait_ge(s_cs[kind], h * 3 + (1 if j == 0 else 2))
                        v.scalar_tensor_tensor(out=cv[kind][:, 0:n], in0=raw[kind][:, j:j + n], scalar=tap(j, kind, h),
                                               in1=cv[kind][:, 0:n], op0=ALU.mult, op1=ALU.add).then_inc(s_cs[kind], 1)

                def unit(kind, h):
                    v.wait_ge(s_bank[kind], h + 2)
                    for c0, n in ((0, LAT), (CTX_AT, CTX))[:1 + kind]:
                        ri = v.reciprocal(crn[:, c0:c0 + n], crn[:, c0:c0 + n])
                    ri.then_inc(s_cri[kind], 1)
                    v.wait_ge(s_cri[kind], h + 1)
                    dst = (qT, kT)[kind]
                    for c0, n in ((0, LAT), (CTX_AT, CTX))[:1 + kind]:
                        mu = v.scalar_tensor_tensor(out=dst[:, at(h, 1), c0:c0 + n].rearrange("p a n -> p (a n)"), in0=cv[kind][:, c0:c0 + n],
                                                    scalar=(P ** -0.5 if kind == 0 else 1.0), in1=crn[:, c0:c0 + n],
                                                    op0=ALU.mult, op1=ALU.mult)
                    if kind == 0:
                        mu.then_inc(s_qu, 1)

                def copy_v(h):
                    v.wait_ge(s_vtt, h + 1)
                    for b, n in ((0, 4), (1, 4), (2, 2)):
                        cp = v.tensor_copy(vtok[:, 4 * b:4 * b + n, at(h * P, P)],
                                           PS[:, 5 + b, 0:n * P].rearrange("p (c n) -> p c n", c=n))
                    cp.then_inc(s_bank[2], 1)

                def head(h, last_v):
                    conv(0, h)
                    if last_v is not None:
                        copy_v(last_v)
                    conv(1, h)
                    unit(0, h)
                    conv(2, h)
                    unit(1, h)
                head(0, None)
                with v.Fori(1, H) as h:
                    head(h, h - 1)
                copy_v(H - 1)
                v.wait_ge(s_lt, 1)
                v.tensor_copy(ab[:, :, :], PS[:, 3, 0:480].rearrange("p (c n) -> p c n", c=NT)[:, :, 32:48]).then_inc(s_gd, 1)
                v.wait_ge(s_gd, 1)
                v.wait_ge(s_hb, 32)
                v.tensor_tensor(gtmp[:, 0, :, :], ab[:, :, 0:8], hbias[:, 0, :].unsqueeze(1).to_broadcast([P, NT, 8]),
                                ALU.add).then_inc(s_gd, 1)
                v.wait_ge(s_ga, 4)
                v.scalar_tensor_tensor(out=gtmp[:, 0, :, :], in0=gtmp[:, 0, :, :], scalar=0.0, in1=gtmp[:, 1, :, :],
                                       op0=ALU.max, op1=ALU.add).then_inc(s_pad, 1)
                v.wait_ge(s_pad, 2)
                v.scalar_tensor_tensor(out=gdec[:, :, :], in0=gtmp[:, 0, :, :], scalar=-1.0,
                                       in1=hbias[:, 1, :].unsqueeze(1).to_broadcast([P, NT, 8]),
                                       op0=ALU.mult, op1=ALU.mult).then_inc(s_gd, 1)
                v.wait_ge(s_gm, 1)
                v.tensor_copy(gsum[:, :, :, :].rearrange("p a b n -> p (a b n)"), PS[:, 4, 0:160]).then_inc(s_gd, 1)
                v.wait_ge(s_ga, 6)
                v.tensor_scalar(nbeta[:, :, :], beta[:, :, :], -1.0, None, ALU.mult).then_inc(s_pad, 1)
                v.wait_ge(s_pad, 3)
                for d in range(2):
                    v.tensor_tensor(nbe[:, d, :].rearrange("p (c h) -> p c h", h=H), nbeta[:, :, 4 * d:4 * d + 4],
                                    gexp[:, 0, d, :].rearrange("p (c h) -> p c h", h=H), ALU.mult)

        if stop == 1:
            return


        spots = [55 + 2 * i for i in range(15)] + [143 + 2 * i for i in range(16)] + [197 + 2 * i for i in range(5)]

        def pair(name):
            return [place(f"{name}{d}", [P, HW], spots.pop(0)) for d in range(2)]
        kS, gB, E, dA, dN, N, NTs, X, XT, Ys = [pair(n) for n in ("kS", "gB", "E", "dA", "dN", "N", "NTs", "X", "XT", "Ys")]
        QeT, vB, kBe, Kd, WTs, Vn, S = [pair(n) for n in ("QeT", "vB", "kBe", "Kd", "WTs", "Vn", "S")]
        og = place("og", [P, NL, HW], 176)

        def two(name):
            return [sem(f"{name}_f"), sem(f"{name}_b")]
        s_ks, s_gb, s_gc, s_kk, s_kt = two("k_staged"), two("g_spread"), two("g_rows"), two("kk_kq"), two("k_turned")
        s_dm, s_exp, s_e = two("decay_args"), two("decays"), two("exp_rows")
        s_dc, s_n, s_ntp, s_nts = two("decay_arg_step"), two("n_ready"), two("n_turned"), two("nt_copied")
        s_xi0, s_x, s_xT = two("x_identity"), two("x_ready"), two("xt_ready")
        s_y, s_ys, s_p, s_pt = two("y_product"), two("y_copied"), two("p_product"), two("pt_product")
        s_at, s_atm, s_qe, s_vb = two("at_ready"), two("at_masked"), two("q_decayed"), two("v_beta")
        s_wt, s_wts, s_vn, s_vns, s_o, s_u = two("w_product"), two("w_copied"), two("vnew_product"), two("vnew_copied"), two("o_product"), two("u_product")
        s_s, s_og, s_tick = two("state"), sem("o_zeroed"), sem("masked_copy_tick")
        s_dmin = two("a_decay_args")
        NLV = LEVELS - 1

        def chunk(d, i, lat):
            if lat:
                c = i if d == 0 else i * -1 + (NL - 1)
                return c, c * P
            c = NL + (i if d == 0 else NC - 1 - i)
            return c, c * P + 1

        def scan(eng, body):
            for i in range(NC):
                body(i, i, False)
            with eng.Fori(0, NL) as i:
                body(i, i + NC, True)

        with nc.Block() as block:
            @block.tensor
            def _(pe):
                def hd(b, h):
                    return PS[:, b, h * P:(h + 1) * P]

                def hs(tile, h):
                    return tile[:, h * P:(h + 1) * P]

                def four(bank, lhs, rhs, sem_):
                    for h in range(H):
                        mm = pe.matmul(hd(bank, h), lhs(h), rhs(h), start=True, stop=True)
                    mm.then_inc(sem_, 1)

                def body(i, t, lat):
                    for d in range(2):
                        c, at_ = chunk(d, i, lat)
                        b = 4 * d
                        pe.wait_ge(s_gb[d], t + 1)
                        four(b + 2, lambda h: hs(gB[d], h), lambda h: tri[:, d, :], s_gc[d])
                        pe.wait_ge(s_ks[d], t + 1)
                        four(b, lambda h: hs(kS[d], h), lambda h: hs(kS[d], h), s_kk[d])
                        if lat:
                            four(b + 1, lambda h: hs(kS[d], h), lambda h: qT[:, h, at(at_, P)], s_kk[d])
                        for h in range(H):
                            tr = pe.transpose(hd(b + 3, h), hs(kS[d], h), ident[:, :])
                        tr.then_inc(s_kt[d], 1)
                    for d in range(2):
                        b = 4 * d
                        pe.wait_ge(s_n[d], t + 1)
                        for h in range(H):
                            tr = pe.transpose(hd(b + 2, h), hs(N[d], h), ident[:, :])
                        tr.then_inc(s_ntp[d], 1)
                    for l in range(1, LEVELS):
                        for d in range(2):
                            b = 4 * d
                            if l == 1:
                                pe.wait_ge(s_nts[d], t + 1)
                            pe.wait_ge(s_x[d], t * NLV + l)
                            four(b, lambda h: hs(NTs[d], h), lambda h: hs(X[d], h), s_y[d])
                        for d in range(2):
                            b = 4 * d
                            pe.wait_ge(s_ys[d], t * NLV + l)
                            pe.wait_ge(s_xT[d], t * LEVELS + l)
                            four(b + 2, lambda h: hs(Ys[d], h), lambda h: hs(XT[d], h), s_pt[d])
                        for d in range(2):
                            if l < NLV:
                                pe.wait_ge(s_xT[d], t * LEVELS + (l + 1))
                                for h in range(H):
                                    tr = pe.transpose(hd(4 * d + 1, h), hs(XT[d], h), ident[:, :])
                                tr.then_inc(s_p[d], 1)
                    for d in range(2):
                        pe.wait_ge(s_xT[d], (t + 1) * LEVELS)
                        four(4 * d, lambda h: hs(kBe[d], h), lambda h: hs(XT[d], h), s_wt[d])
                    for d in range(2):
                        b = 4 * d
                        pe.wait_ge(s_vb[d], t + 1)
                        pe.wait_ge(s_wts[d], t + 1)
                        pe.wait_ge(s_s[d], t + 1)
                        for h in range(H):
                            pe.matmul(hd(b + 1, h), hs(XT[d], h), hs(vB[d], h), start=True, stop=False)
                            mm = pe.matmul(hd(b + 1, h), hs(WTs[d], h), hs(S[d], h), start=False, stop=True)
                        mm.then_inc(s_vn[d], 1)
                    for d in range(2):
                        b = 4 * d
                        pe.wait_ge(s_vns[d], t + 1)
                        four(b + 3, lambda h: hs(Kd[d], h), lambda h: hs(Vn[d], h), s_u[d])
                        if lat:
                            pe.wait_ge(s_qe[d], i + 1)
                            pe.wait_ge(s_atm[d], i + 1)
                            for h in range(H):
                                pe.matmul(hd(b + 2, h), hs(QeT[d], h), hs(S[d], h), start=True, stop=False)
                                mm = pe.matmul(hd(b + 2, h), hs(dA[d], h), hs(Vn[d], h), start=False, stop=True)
                            mm.then_inc(s_o[d], 1)
                scan(pe, body)

            @block.scalar
            def _(a):
                def body(i, t, lat):
                    for d in range(2):
                        a.wait_ge(s_gc[d], t + 1)
                        a.activation(E[d][:, :], PS[:, 4 * d + 2, :], ACT.Exp).then_inc(s_e[d], 1)
                        a.wait_ge(s_dm[d], t + 1)
                        a.activation(dN[d][:, :], dN[d][:, :], ACT.Exp, scale=-1.0).then_inc(s_exp[d], 1)
                    if lat:
                        for d in range(2):
                            a.wait_ge(s_dmin[d], i + 1)
                            a.activation(dA[d][:, :], dA[d][:, :], ACT.Exp).then_inc(s_exp[d], 1)
                    for d in range(2):
                        a.wait_ge(s_ntp[d], t + 1)
                        a.activation(NTs[d][:, :], PS[:, 4 * d + 2, :], ACT.Copy).then_inc(s_nts[d], 1)
                    for l in range(1, LEVELS):
                        for d in range(2):
                            a.wait_ge(s_y[d], t * NLV + l)
                            a.activation(half(Ys[d][:, :], 1 << l, d), half(PS[:, 4 * d, :], 1 << l, d), ACT.Copy).then_inc(s_ys[d], 1)
                        for d in range(2):
                            if l < NLV:
                                a.wait_ge(s_p[d], t * (NLV - 1) + l)
                                a.activation(half(X[d][:, :], 1 << l, d), half(PS[:, 4 * d + 1, :], 1 << l, d), ACT.Copy).then_inc(s_x[d], 1)
                    for d in range(2):
                        a.wait_ge(s_wt[d], t + 1)
                        a.activation(WTs[d][:, :], PS[:, 4 * d, :], ACT.Copy).then_inc(s_wts[d], 1)
                    for d in range(2):
                        a.wait_ge(s_vn[d], t + 1)
                        a.activation(Vn[d][:, :], PS[:, 4 * d + 1, :], ACT.Copy).then_inc(s_vns[d], 1)
                scan(a, body)

            @block.gpsimd
            def _(g):
                g.memset(og[:, :, :], 0.0).then_inc(s_og, 1)
                ident4 = ident[:, :].unsqueeze(1).to_broadcast([P, H, P])
                ones4 = ones[:, :].unsqueeze(1).to_broadcast([P, H, P])

                def body(i, t, lat):
                    for d in range(2):
                        c, at_ = chunk(d, i, lat)
                        g.wait_ge(s_e[d], t + 1)
                        for m in (X, XT):
                            cp = g.tensor_tensor(heads(m[d][:, :]), ident4, ones4, ALU.mult)
                        cp.then_inc(s_xi0[d], 1)
                        if lat:
                            g.tensor_tensor(heads(QeT[d][:, :]), qT[:, :, at(at_, P)], heads(E[d][:, :]), ALU.mult).then_inc(s_qe[d], 1)
                        g.tensor_tensor(heads(vB[d][:, :]), vtok[:, at(c, 1), :].rearrange("p a (h n) -> p (a h) n", h=H),
                                        beta[:, at(c, 1), 4 * d:4 * d + 4].rearrange("p a h -> p (a h)").unsqueeze(2).to_broadcast([P, H, P]),
                                        ALU.mult).then_inc(s_vb[d], 1)
                    if lat:
                        for d in range(2):
                            g.wait_ge(s_at[d], i + 1)
                            g.tensor_tensor(heads(dA[d][:, :]), heads(dA[d][:, :]),
                                            tri[:, d, :].unsqueeze(1).to_broadcast([P, H, P]), ALU.mult).then_inc(s_atm[d], 1)
                scan(g, body)

            @block.vector
            def _(v):
                for d in range(2):
                    v.memset(Ys[d][:, :], 0.0)
                    v.memset(S[d][:, :], 0.0).then_inc(s_s[d], 1)
                v.wait_ge(s_og, 1)

                def masked_wait(*waits):
                    for sm, n in waits:
                        v.wait_ge(sm, n)
                    v.sem_inc(s_tick, 1)

                def merge(dst, l, side, src, sem_):
                    def cols(ap):
                        return ap.rearrange("p (q b h x) -> p q b h x", q=H, h=2, x=1 << l)[:, :, :, side, :]
                    mask = half(quad[:, side, l, :], 1 << l, side).unsqueeze(1)
                    v.copy_predicated(cols(dst[:, :]), mask.to_broadcast([P, H, 64 >> l, 1 << l]), cols(src)).then_inc(sem_, 1)

                def body(i, t, lat):
                    for d in range(2):
                        c, at_ = chunk(d, i, lat)
                        v.tensor_copy(heads(gB[d][:, :]), gdec[:, at(c, 1), 4 * d:4 * d + 4].rearrange("p a h -> p (a h)").unsqueeze(2)
                                      .to_broadcast([P, H, P])).then_inc(s_gb[d], 1)
                        v.tensor_copy(heads(kS[d][:, :]), kT[:, :, at(at_, P)]).then_inc(s_ks[d], 1)
                    for d in range(2):
                        c, at_ = chunk(d, i, lat)
                        v.wait_ge(s_e[d], t + 1)
                        v.tensor_tensor(heads(dA[d][:, :]), heads(PS[:, 4 * d + 2, :]), bc(gsum[:, 0, d, at(c * H, H)], P),
                                        ALU.subtract).then_inc(s_dc[d], 1)
                        v.wait_ge(s_dc[d], t + 1)
                        v.tensor_scalar(dN[d][:, :], dA[d][:, :], 0.0, None, ALU.max).then_inc(s_dm[d], 1)
                    if lat:
                        for d in range(2):
                            v.wait_ge(s_dm[d], t + 1)
                            v.tensor_scalar(dA[d][:, :], dA[d][:, :], 0.0, None, ALU.min).then_inc(s_dmin[d], 1)
                    for d in range(2):
                        c, at_ = chunk(d, i, lat)
                        v.wait_ge(s_kk[d], (2 * t - NC + 1) if lat else t + 1)
                        v.wait_ge(s_exp[d], (2 * t - NC + 1) if lat else t + 1)
                        for h in range(H):
                            n = v.scalar_tensor_tensor(out=N[d][:, h * P:(h + 1) * P], in0=PS[:, 4 * d, h * P:(h + 1) * P],
                                                       scalar=nbeta[:, at(c, 1), 4 * d + h:4 * d + h + 1].rearrange("p a h -> p (a h)"),
                                                       in1=dN[d][:, h * P:(h + 1) * P], op0=ALU.mult, op1=ALU.mult)
                        n.then_inc(s_n[d], 1)
                    for d in range(2):
                        masked_wait((s_xi0[d], t + 1), (s_n[d], t + 1))
                        merge(X[d], 0, d, N[d][:, :], s_x[d])
                        masked_wait((s_nts[d], t + 1))
                        merge(XT[d], 0, 1 - d, PS[:, 4 * d + 2, :], s_xT[d])
                    if lat:
                        for d in range(2):
                            v.wait_ge(s_kk[d], 2 * t - NC + 2)
                            v.wait_ge(s_exp[d], 2 * t - NC + 2)
                            v.tensor_tensor(dA[d][:, :], PS[:, 4 * d + 1, :], dA[d][:, :], ALU.mult).then_inc(s_at[d], 1)
                    for l in range(1, LEVELS):
                        for d in range(2):
                            masked_wait((s_pt[d], t * NLV + l))
                            merge(XT[d], l, 1 - d, PS[:, 4 * d + 2, :], s_xT[d])
                        if l <= 2:
                            d = l - 1
                            c, at_ = chunk(d, i, lat)
                            v.wait_ge(s_kt[d], t + 1)
                            v.tensor_tensor(heads(kBe[d][:, :]), heads(PS[:, 4 * d + 3, :]), bc(nbe[:, d, at(c * H, H)], P), ALU.mult)
                            v.tensor_tensor(heads(Kd[d][:, :]), heads(PS[:, 4 * d + 3, :]), bc(gexp[:, 1, d, at(c * H, H)], P), ALU.mult)
                    for d in range(2):
                        c, at_ = chunk(d, i, lat)
                        last = P - 1 if d == 0 else 0
                        v.wait_ge(s_u[d], t + 1)
                        if lat:
                            v.wait_ge(s_o[d], i + 1)
                            v.tensor_tensor(og[:, at(c, 1), :].rearrange("p a n -> p (a n)"), PS[:, 4 * d + 2, :],
                                            og[:, at(c, 1), :].rearrange("p a n -> p (a n)"), ALU.add)
                        for h in range(H):
                            st = v.scalar_tensor_tensor(out=S[d][:, h * P:(h + 1) * P], in0=S[d][:, h * P:(h + 1) * P],
                                                        scalar=E[d][:, h * P + last:h * P + last + 1],
                                                        in1=PS[:, 4 * d + 3, h * P:(h + 1) * P], op0=ALU.mult, op1=ALU.add)
                        st.then_inc(s_s[d], 1)
                        v.wait_ge(s_s[d], t + 2)
                scan(v, body)

        if stop == 2:
            return


        recycle()

        ws = [place(f"ws{i}", [P, KT, P], 55 + 4 * i) for i in range(2)]
        gz = [place(f"gz{i}", [P, TOK], 63 + 5 * i) for i in range(2)]
        ga = [place(f"ga{i}", [P, TOK], 73 + 5 * i) for i in range(2)]
        cmask = place("cmask", [P, TOK], 83, BF16)
        gq = place("gq", [P, 2, LAT], 86)
        gk = place("gk", [P, 2, TOK], 94)
        gvtok = place("gvtok", [P, NT, HW], 104)
        gP = place("gP", [P, 2, 2, TOK], 124)
        sz = place("sz", [P, 2 * H, LAT], 144)
        graw = [place(f"graw{i}", [P, TOK], 197 + 5 * i) for i in range(2)]

        s_cm = sem("chunk_mask")
        s_w3 = [sem(f"w3_in{i}") for i in range(2)]
        s_m3 = sem("tile3_product")
        s_b3 = [sem(f"tile3_banks_free{i}") for i in range(2)]
        s_gr = sem("gv_copied")
        s_gvt = sem("gv_turned")
        s_zm, s_zc = sem("decay_product"), sem("decay_input")
        s_za, s_zs, s_zf = sem("decay_act"), sem("decay_step"), sem("decay_sums")

        N_G, N_V, N_QK, N_ALL = H, 2 * H, 3 * H, 4 * H

        with nc.Block() as block:
            @block.sync
            def _(sp):
                def load(n, u, col, first):
                    if not first:
                        sp.wait_ge(s_m3, n - 1)
                    sp.dma_start(ws[u][:, :, :], win[:, :, at(col, P)]).then_inc(s_w3[u], 16)

                def run(first, n, col0):
                    steps(sp, first, n, lambda n_, u: load(n_, u, n_ * P + (col0 - first * P), False))
                load(0, 0, Z0, True)
                load(1, 1, Z0 + P, True)
                run(2, 2, Z0 + 2 * P)
                run(N_G, H, GG0)
                run(N_V, H, GV0)
                run(N_QK, H, GQ0)

            @block.tensor
            def _(pe):
                for j in range(4):
                    d, p = divmod(j, 2)
                    for b, (t0, n) in enumerate(PARTS[1]):
                        m = 3 * j + b
                        if m >= 2:
                            pe.wait_ge(s_zc, m - 1)
                        pe.matmul(PS[:, 6 + m % 2, 0:n], wgk[:, d, p * P:(p + 1) * P], lrab[0:32, t0:t0 + n],
                                  start=True, stop=True).then_inc(s_zm, 1)

                def pairs(first, n, parts, after=None):
                    def two_tiles(i):
                        for u in range(2):
                            pe.wait_ge(s_w3[u], i * 16 + (8 * first + 16))
                            pe.wait_ge(s_b3[u], i + (first // 2 + 1))
                            for b, (t0, w) in enumerate(parts):
                                for k in range(KT):
                                    mm = pe.matmul(PS[:, 3 * u + b, 0:w], ws[u][:, k, :], hT[:, k, t0:t0 + w],
                                                   start=(k == 0), stop=(k == KT - 1))
                            mm.then_inc(s_m3, 1)
                        if after:
                            for u in range(2):
                                after(i, u)
                    with pe.Fori(0, n // 2) as i:
                        two_tiles(i)

                def turn(i, u):
                    pe.wait_ge(s_gr, i * 2 + (u + 1))
                    for ch in range(NT):
                        tr = pe.transpose(PS[:, 3 * u + ch // 4, (ch % 4) * P:(ch % 4 + 1) * P],
                                          graw[u][:, ch * P:(ch + 1) * P], ident[:, :])
                    tr.then_inc(s_gvt, 1)
                pairs(0, N_V, PARTS[0])
                pairs(N_V, H, PARTS[1], turn)
                for j in range(4):
                    n, u = N_QK + j, j % 2
                    pe.wait_ge(s_w3[u], 8 * n + 16 - 8 * u)
                    pe.wait_ge(s_b3[u], n // 2 + 1)
                    for b, (t0, w) in enumerate(PARTS[j // 2]):
                        for k in range(KT):
                            mm = pe.matmul(PS[:, 3 * u + b, 0:w], ws[u][:, k, :], hT[:, k, t0:t0 + w],
                                           start=(k == 0), stop=(k == KT - 1))
                    mm.then_inc(s_m3, 1)

            @block.scalar
            def _(a):
                a.sem_inc(s_b3[0], 1)
                a.sem_inc(s_b3[1], 1)

                def decay(j):
                    if j >= 2:
                        a.wait_ge(s_zf, j - 1)
                    for b, (t0, n) in enumerate(PARTS[1]):
                        m = 3 * j + b
                        a.wait_ge(s_zm, m + 1)
                        a.activation(gz[j % 2][:, t0:t0 + n], PS[:, 6 + m % 2, 0:n], ACT.Identity,
                                     bias=vcol[:, BGK + j:BGK + j + 1]).then_inc(s_zc, 1)
                    a.wait_ge(s_zc, 3 * j + 3)
                    a.activation(ga[j % 2][:, :], gz[j % 2][:, :], ACT.Abs).then_inc(s_za, 1)
                    a.wait_ge(s_za, 3 * j + 1)
                    a.activation(ga[j % 2][:, :], ga[j % 2][:, :], ACT.Exp, scale=-1.0).then_inc(s_za, 1)
                    a.wait_ge(s_za, 3 * j + 2)
                    a.activation(ga[j % 2][:, :], ga[j % 2][:, :], ACT.Ln, bias=1.0).then_inc(s_za, 1)
                for j in range(4):
                    decay(j)

                def silu(base, first, n):
                    def body(i, u):
                        a.wait_ge(s_m3, i + (first + 1))
                        a.activation(sz[:, at(i + base, 1), :].rearrange("p a n -> p (a n)"),
                                     PS[:, 3 * u:3 * u + 2, :].rearrange("p a n -> p (a n)"), ACT.Silu).then_inc(s_b3[u], 1)
                    steps(a, 0, n, body)
                silu(0, 0, N_V)

                def copy_v(i, u):
                    a.wait_ge(s_m3, i + (N_V + 1))
                    a.activation(graw[u][:, 0:LAT], PS[:, 3 * u:3 * u + 2, :].rearrange("p a n -> p (a n)"), ACT.Copy)
                    a.activation(graw[u][:, LAT:TOK], PS[:, 3 * u + 2, 0:CTX], ACT.Copy).then_inc(s_gr, 1)
                steps(a, 0, H, copy_v)
                for j in range(4):
                    u = j % 2
                    a.wait_ge(s_m3, N_QK + j + 1)
                    src = PS[:, 3 * u:3 * u + 2, :].rearrange("p a n -> p (a n)")
                    if j < 2:
                        a.activation(gq[:, j, :], src, ACT.Copy, scale=(P // 2) ** -0.5).then_inc(s_b3[u], 1)
                    else:
                        a.activation(gk[:, j - 2, 0:LAT], src, ACT.Copy)
                        a.activation(gk[:, j - 2, LAT:TOK], PS[:, 3 * u + 2, 0:CTX], ACT.Copy).then_inc(s_b3[u], 1)

            @block.vector
            def _(v):
                v.memset(cmask[:, :], 1.0).then_inc(s_cm, 1)
                v.wait_ge(s_cm, 1)
                v.memset(cmask[:, 0:TOK:P], 0.0).then_inc(s_cm, 1)
                v.wait_ge(s_cm, 2)
                for j in range(4):
                    d, p = divmod(j, 2)
                    z, s = gz[j % 2], ga[j % 2]
                    v.wait_ge(s_za, 3 * j + 3)
                    v.scalar_tensor_tensor(out=z[:, :], in0=z[:, :], scalar=0.0, in1=s[:, :], op0=ALU.min,
                                           op1=ALU.subtract).then_inc(s_zs, 1)
                    v.wait_ge(s_zs, 2 * j + 1)
                    zv, sv = (z[:, :], s[:, :]) if d == 0 else (z[:, ::-1], s[:, ::-1])
                    v.tensor_tensor_scan(sv, cmask[:, :], zv, 0.0, ALU.mult, ALU.add).then_inc(s_zs, 1)
                    v.wait_ge(s_zs, 2 * j + 2)
                    v.tensor_scalar(gP[:, d, p, :], s[:, :], 1.0 / 16, None, ALU.mult).then_inc(s_zf, 1)

                def copy_v(i, u):
                    v.wait_ge(s_gvt, i + 1)
                    for b, n in ((0, 4), (1, 4), (2, 2)):
                        cp = v.tensor_copy(gvtok[:, 4 * b:4 * b + n, at(i * P, P)],
                                           PS[:, 3 * u + b, 0:n * P].rearrange("p (c n) -> p c n", c=n))
                    cp.then_inc(s_b3[u], 1)
                steps(v, 0, H, copy_v)

        if stop == 3:
            return


        og2 = place("og2", [P, NL, HW], 15)
        Ex = [place(f"Ex{i}", [P, 2, 2, P], 31 + 2 * i) for i in range(2)]
        Qbd = [place(f"Qbd{i}", [P, 2, 2, P], 35 + 2 * i) for i in range(2)]
        Kt = [place(f"Kt{i}", [P, 2, P], 39 + i) for i in range(2)]
        AT = place("AT", [P, HW], 41)
        Eq = [place(f"Eq{i}", [P, 2, P], 43 + i) for i in range(2)]
        Qe = [place(f"Qe{i}", [P, 2, P], 45 + i) for i in range(2)]
        Ek = [place(f"Ek{i}", [P, 2, P], 47 + i) for i in range(2)]
        Kde = [place(f"Kde{i}", [P, 2, P], 49 + i) for i in range(2)]
        Kdt = [place(f"Kdt{i}", [P, 2, P], 51 + i) for i in range(2)]
        Sbd = [place(f"Sbd{i}", [P, 2, 2, P], 53 + 2 * i) for i in range(2)]

        s_z4, s_tk4 = sem("gla_zeroed"), sem("gla_masked_tick")
        s_tkg, s_tk5, s_tk6 = sem("gla_pool_tick"), sem("residual_tick"), sem("gated_product_tick")
        s_lq, s_lk, s_lx = sem("level_q_args"), sem("level_k_args"), sem("level_factors")
        s_lQ, s_lK, s_lp, s_lm = sem("level_q"), sem("level_k"), sem("level_product"), sem("level_merged")
        s_de, s_da, s_dk = two("gla_q_factor"), two("gla_k_arg"), two("gla_k_factor")
        s_qe2, s_kde, s_t2, s_kd2 = two("gla_q"), two("gla_k"), two("gla_k_turned"), two("gla_k_copied")
        s_o2, s_u2, s_s2 = two("gla_o"), two("gla_u"), two("gla_state")
        s_og2 = sem("o_of_backward_added")
        ND = LEVELS + 1

        def cols(d, i, lat):
            if lat:
                c = i if d == 0 else i * -1 + (NL - 1)
            else:
                c = NL + (i if d == 0 else NC - 1 - i)
            return c, c * P

        with nc.Block() as block:
            @block.tensor
            def _(pe):
                def level(i, l):
                    u = l % 2
                    pe.wait_ge(s_lQ, i * ND + (l + 1))
                    if l < LEVELS:
                        pe.wait_ge(s_lK, i * LEVELS + (l + 2))
                    for p in range(2):
                        mm = pe.matmul(PS[:, u, 2 * p * P:2 * (p + 1) * P], Kt[u][:, p, :],
                                       Qbd[u][:, p, :, :].rearrange("p a n -> p (a n)"), start=True, stop=True)
                    mm.then_inc(s_lp, 1)

                def body(i, t, lat):
                    if lat:
                        for l in range(LEVELS):
                            level(i, l)
                    for d in range(2):
                        pe.wait_ge(s_kde[d], t + 1)
                        for p in range(2):
                            tr = pe.transpose(PS[:, 2 + d, p * P:(p + 1) * P], Kde[d][:, p, :], ident[:, :])
                        tr.then_inc(s_t2[d], 1)
                    if lat:
                        for d in range(2):
                            pe.wait_ge(s_qe2[d], i + 1)
                            pe.wait_ge(s_s2[d], t + 1)
                            for p in range(2):
                                mm = pe.matmul(PS[:, 4 + d, 2 * p * P:2 * (p + 1) * P], Qe[d][:, p, :],
                                               Sbd[d][:, p, :, :].rearrange("p a n -> p (a n)"), start=(p == 0), stop=(d == 1),
                                               skip_group_check=True)
                        mm.then_inc(s_o2[1], 1)
                        level(i, LEVELS)
                    for d in range(2):
                        c, at_ = cols(d, i, lat)
                        pe.wait_ge(s_kd2[d], t + 1)
                        for p in range(2):
                            mm = pe.matmul(PS[:, 6 + d, 2 * p * P:2 * (p + 1) * P], Kdt[d][:, p, :],
                                           gvtok[:, at(c, 1), 2 * p * P:2 * (p + 1) * P].rearrange("p a n -> p (a n)"),
                                           start=True, stop=True)
                        mm.then_inc(s_u2[d], 1)
                    if lat:
                        c, at_ = cols(0, i, lat)
                        pe.wait_ge(s_lm, i * ND + ND)
                        for h in range(H):
                            mm = pe.matmul(PS[:, 4, h * P:(h + 1) * P], AT[:, h * P:(h + 1) * P],
                                           gvtok[:, at(c, 1), h * P:(h + 1) * P].rearrange("p a n -> p (a n)"),
                                           start=False, stop=True, skip_group_check=True)
                        mm.then_inc(s_o2[0], 1)
                scan(pe, body)

            @block.scalar
            def _(a):
                def q_factor(d, i, t, lat):
                    c, at_ = cols(d, i, lat)
                    a.wait_ge(s_s2[d], t + 1)
                    a.activation(Eq[d][:, :, :], gP[:, d, :, at(at_, P)], ACT.Exp).then_inc(s_de[d], 1)

                def k_factor(d, t):
                    a.wait_ge(s_da[d], t + 1)
                    a.activation(Ek[d][:, :, :], Ek[d][:, :, :], ACT.Exp).then_inc(s_dk[d], 1)

                def body(i, t, lat):
                    for l in range(LEVELS):
                        if lat:
                            a.wait_ge(s_lq, i * LEVELS + (l + 1))
                            a.wait_ge(s_lk, i * LEVELS + (l + 1))
                            e = Ex[l % 2][:, :, :, :]
                            a.activation(e, e, ACT.Exp).then_inc(s_lx, 1)
                        if l == 1:
                            for d in range(2):
                                q_factor(d, i, t, lat)
                        if l == 3:
                            for d in range(2):
                                k_factor(d, t)
                    for d in range(2):
                        a.wait_ge(s_t2[d], t + 1)
                        a.activation(Kdt[d][:, :, :].rearrange("p a n -> p (a n)"), PS[:, 2 + d, 0:2 * P], ACT.Copy).then_inc(s_kd2[d], 1)
                scan(a, body)

            def halves(ap, m):
                return ap.rearrange("p t (b h x) -> p t b h x", h=2, x=m)

            def borders(gp, d, m, nb):
                v = halves(gp, m)
                e = v[:, :, :, 0, m - 1] if d == 0 else v[:, :, :, 1, 0]
                return e.unsqueeze(3).to_broadcast([P, 2, nb, m])

            @block.gpsimd
            def _(g):
                g.memset(og2[:, :, :], 0.0).then_inc(s_z4, 1)
                g.sem_inc(s_lK, 1)
                g.sem_inc(s_lp, 1)

                def k_args(i, t, lat):
                    for d in range(2):
                        c, at_ = cols(d, i, lat)
                        last = at_ + (P - 1 if d == 0 else 0)
                        if lat or i:
                            g.wait_ge(s_kde[d], t)
                            g.sem_inc(s_tkg, 1)
                        g.tensor_tensor(Ek[d][:, :, :], gP[:, d, :, at(last, 1)].to_broadcast([P, 2, P]),
                                        gP[:, d, :, at(at_, P)], ALU.subtract).then_inc(s_da[d], 1)

                def decayed(i, t, lat):
                    for d in range(2):
                        c, at_ = cols(d, i, lat)
                        g.wait_ge(s_dk[d], t + 1)
                        g.sem_inc(s_tkg, 1)
                        g.tensor_tensor(Kde[d][:, :, :], gk[:, :, at(at_, P)], Ek[d][:, :, :], ALU.mult).then_inc(s_kde[d], 1)
                        if lat:
                            g.wait_ge(s_de[d], t + 1)
                            g.sem_inc(s_tkg, 1)
                            g.tensor_tensor(Qe[d][:, :, :], gq[:, :, at(at_, P)], Eq[d][:, :, :], ALU.mult).then_inc(s_qe2[d], 1)

                def body(i, t, lat):
                    if not lat:
                        k_args(i, t, lat)
                        decayed(i, t, lat)
                        return
                    gf, gb, kk = (gP[:, 0, :, at(i * P, P)], gP[:, 1, :, at(i * P, P)], gk[:, :, at(i * P, P)])
                    for l in range(LEVELS + 1):
                        if l < LEVELS:
                            m = 1 << (LEVELS - 1 - l)
                            nb = P // (2 * m)
                            e = halves(Ex[l % 2][:, 1, :, :], m)
                            g.wait_ge(s_lK, i * LEVELS + max(l, 1))
                            g.sem_inc(s_tkg, 1)
                            g.tensor_tensor(e[:, :, :, 0, :], borders(gf, 0, m, nb), halves(gf, m)[:, :, :, 0, :], ALU.subtract)
                            g.tensor_tensor(e[:, :, :, 1, :], borders(gb, 1, m, nb), halves(gb, m)[:, :, :, 1, :],
                                            ALU.subtract).then_inc(s_lk, 1)
                        if l >= 1:
                            g.wait_ge(s_lx, i * LEVELS + l)
                            g.wait_ge(s_lp, i * ND + max(l - 1, 1))
                            g.sem_inc(s_tkg, 1)
                            g.tensor_tensor(Kt[(l - 1) % 2][:, :, :], kk, Ex[(l - 1) % 2][:, 1, :, :], ALU.mult).then_inc(s_lK, 1)
                        if l == 2:
                            k_args(i, t, lat)
                        if l == 5:
                            decayed(i, t, lat)
                scan(g, body)

            @block.vector
            def _(v):
                for u in range(2):
                    v.memset(Qbd[u][:, :, :, :], 0.0)
                for d in range(2):
                    v.memset(Sbd[d][:, :, :, :], 0.0).then_inc(s_s2[d], 1)
                v.wait_ge(s_s2[1], 1)
                v.wait_ge(s_s2[0], 1)
                v.wait_ge(s_z4, 1)

                def q_args(l, at_):
                    gf, gb = gP[:, 0, :, at(at_, P)], gP[:, 1, :, at(at_, P)]
                    m = 1 << (LEVELS - 1 - l)
                    nb = P // (2 * m)
                    e = halves(Ex[l % 2][:, 0, :, :], m)
                    v.tensor_tensor(e[:, :, :, 1, :], halves(gf, m)[:, :, :, 1, :], borders(gf, 0, m, nb), ALU.subtract)
                    v.tensor_tensor(e[:, :, :, 0, :], halves(gb, m)[:, :, :, 0, :], borders(gb, 1, m, nb),
                                    ALU.subtract).then_inc(s_lq, 1)

                def add_o(d, i):
                    c, at_ = cols(d, i, True)
                    v.wait_ge(s_o2[d], i + 1)
                    if d == 0:
                        v.wait_ge(s_og2, i + 1)
                    o = og2[:, at(c, 1), :].rearrange("p a n -> p (a n)")
                    ad = v.tensor_tensor(o, PS[:, 4 + d, :], o, ALU.add)
                    ad.then_inc(s_og2, 1) if d else None

                for l in range(2):
                    q_args(l, 0)

                def body(i, t, lat):
                    if lat:
                        kk = gk[:, :, at(i * P, P)]
                        for n in range(ND + 2):
                            if 2 <= n < LEVELS:
                                v.wait_ge(s_lQ, i * ND + (n - 1))
                                q_args(n, i * P)
                            if n == ND + 1:
                                v.wait_ge(s_lQ, i * ND + LEVELS)
                                for l in range(2):
                                    q_args(l, i * P + P)
                            if 1 <= n <= ND:
                                l = n - 1
                                u = l % 2
                                if l < LEVELS:
                                    v.wait_ge(s_lx, i * LEVELS + (l + 1))
                                    for hf in range(2):
                                        r = slice(64 * hf, 64 * hf + 64)
                                        q_ = v.tensor_tensor(Qbd[u][r, :, hf, :], gq[r, :, at(i * P, P)], Ex[u][r, 0, :, :], ALU.mult)
                                else:
                                    v.wait_ge(s_lp, i * ND + l)
                                    for hf in range(2):
                                        r = slice(64 * hf, 64 * hf + 64)
                                        v.tensor_scalar(Qbd[u][r, :, hf, :], gq[r, :, at(i * P, P)], 2.0, None, ALU.mult)
                                    q_ = v.tensor_scalar(Kt[u][:, :, :], kk, 1.0, None, ALU.mult)
                                q_.then_inc(s_lQ, 1)
                            if n >= 2:
                                l = n - 2
                                v.wait_ge(s_lp, i * ND + (l + 2))
                                if l:
                                    v.wait_ge(s_lm, i * ND + l)
                                v.sem_inc(s_tk4, 1)
                                lvl = LEVELS - 1 - l if l < LEVELS else LEVELS
                                v.copy_predicated(heads(AT[:, :]), both[:, lvl, :].unsqueeze(1).to_broadcast([P, H, P]),
                                                  heads(PS[:, l % 2, :])).then_inc(s_lm, 1)
                    if lat:
                        add_o(1, i)
                    for d in range(2):
                        last = P - 1 if d == 0 else 0
                        v.wait_ge(s_u2[d], t + 1)
                        v.wait_ge(s_de[d], t + 1)
                        for p in range(2):
                            for hf in range(2):
                                r = slice(64 * hf, 64 * hf + 64)
                                st = v.scalar_tensor_tensor(out=Sbd[d][r, p, hf, :], in0=Sbd[d][r, p, hf, :],
                                                            scalar=Eq[d][r, p, last:last + 1],
                                                            in1=PS[r, 6 + d, (2 * p + hf) * P:(2 * p + hf + 1) * P],
                                                            op0=ALU.mult, op1=ALU.add)
                        st.then_inc(s_s2[d], 1)
                    for d in range(2):
                        v.wait_ge(s_s2[d], t + 2)
                    if lat:
                        add_o(0, i)
                scan(v, body)

        if stop == 4:
            return

        x1 = place("x1", [P, NL, D], 31)
        x1_dram = nc.dram_tensor("x1_spill", (LAT, D), F32, kind="Internal").ap()
        h2T = place("h2T", [P, KT, LAT], 63)
        wo = place("wo", [P, KT, D], 95)
        xr = [place(f"xr{i}", [P, D], 127 + 4 * i) for i in range(2)]
        ysb = place("ysb", [P, 2 * H, P], 135)
        yT = place("yT", [P, 2 * H, P], 139)
        gbc = place("gbc", [P, D], 192)
        osq = place("osq", [P, 2 * H, P], 197)
        xn2 = place("xn2", [P, D], 201)
        oss = place("oss", [P, 2 * H], 205)
        ort = place("ort", [P, 2 * H], 205.125)
        ors = place("ors", [P, 2 * H], 205.25)
        ss2 = place("ss2", [P, 1], 205.375)
        rt2 = place("rt2", [P, 1], 205.5)
        rs2 = place("rs2", [P, 1], 205.625)

        s_wo = sem("w_out_in")
        s_xr = [sem(f"x_again_in{i}") for i in range(2)]
        s_dg, s_gbm, s_gbc = sem("gate_diagonal"), sem("gate_rows"), sem("gate_spread")
        s_x1s = sem("x1_spilled")
        s_5q, s_5s, s_5r, s_5i, s_5y = sem("head_squares"), sem("head_sums"), sem("head_roots"), sem("head_rstd"), sem("heads_normed")
        s_5t, s_5e, s_5w, s_5x, s_5a = sem("y_turned"), sem("y_gated"), sem("w_out_product"), sem("gated_y"), sem("x1_ready")
        s_5z, s_5rt, s_5ri, s_5n, s_5u = sem("x1_squares"), sem("x1_root"), sem("x1_rstd"), sem("x1_normed"), sem("x1_turned")
        s_5va, s_5vv = sem("h2_by_act"), sem("h2_by_dve")

        with nc.Block() as block:
            @block.sync
            def _(sp):
                wov = w_out[0].rearrange("(k p) n -> p k n", p=P)
                for half in range(2):
                    sp.dma_start(wo[:, :, half * 512:(half + 1) * 512], wov[:, :, half * 512:(half + 1) * 512]).then_inc(s_wo, 16)

                def load(t, u):
                    if not (isinstance(t, int) and t < 2):
                        sp.wait_ge(s_5a, t - 1)
                    sp.dma_start(xr[u][:, :], x_tok[at(t * P, P), :]).then_inc(s_xr[u], 16)
                load(0, 0)
                load(1, 1)
                steps(sp, 2, NL - 2, load)

            @block.tensor
            def _(pe):
                pe.wait_ge(s_dg, 1)
                for k in range(KT):
                    mm = pe.matmul(PS[:, 6 + k // 4, (k % 4) * P:(k % 4 + 1) * P], ones[:, :], osq[:, k, :], start=True, stop=True)
                mm.then_inc(s_gbm, 1)

                def turn1(t):
                    pe.wait_ge(s_5y, t + 1)
                    for h in range(2 * H):
                        tr = pe.transpose(PS[:, h // 4, (h % 4) * P:(h % 4 + 1) * P], ysb[:, h, :], ident[:, :])
                    tr.then_inc(s_5t, 1)

                def project(t):
                    pe.wait_ge(s_5e, t + 1)
                    if isinstance(t, int):
                        pe.wait_ge(s_wo, 32)
                    for half in range(2):
                        for h in range(2 * H):
                            mm = pe.matmul(PS[:, 2 + half, :], yT[:, h, :], wo[:, h, half * 512:(half + 1) * 512],
                                           start=(h == 0), stop=(h == 2 * H - 1))
                    mm.then_inc(s_5w, 1)

                def turn2(t):
                    pe.wait_ge(s_5n, t + 1)
                    for k in range(KT):
                        tr = pe.transpose(PS[:, 4 + k // 4, (k % 4) * P:(k % 4 + 1) * P], xn2[:, k * P:(k + 1) * P], ident[:, :])
                    tr.then_inc(s_5u, 1)
                turn1(0)
                project(0)
                turn1(1)
                with pe.Fori(1, NL - 1) as t:
                    project(t)
                    turn1(t + 1)
                    turn2(t - 1)
                project(NL - 1)
                turn2(NL - 2)
                turn2(NL - 1)

            @block.scalar
            def _(a):
                def squares(t):
                    if not (isinstance(t, int) and t == 0):
                        a.wait_ge(s_5s, t)
                    else:
                        a.wait_ge(s_gbm, 1)
                    for g_, o in enumerate((og, og2)):
                        sq = a.activation(osq[:, g_ * H:(g_ + 1) * H, :].rearrange("p h n -> p (h n)"),
                                          o[:, at(t, 1), :].rearrange("p a n -> p (a n)"), ACT.Square)
                    sq.then_inc(s_5q, 1)
                    a.wait_ge(s_5s, t + 1)
                    a.activation(ort[:, :], oss[:, :], ACT.Sqrt, scale=1.0 / P, bias=epsc[:, :]).then_inc(s_5r, 1)

                def evac(t):
                    a.wait_ge(s_5u, t + 1)
                    for k in range(4):
                        ev = a.activation(h2T[:, k, at(t * P, P)], PS[:, 4, k * P:(k + 1) * P], ACT.Identity,
                                          scale=gain[:, 2 * KT + k:2 * KT + k + 1], bias=mods[:, 3 * KT + k, 0:1])
                    ev.then_inc(s_5va, 1)

                def second(t):
                    a.wait_ge(s_5a, t + 1)
                    a.activation(osq[:, :, :].rearrange("p h n -> p (h n)"), x1[:, at(t, 1), :].rearrange("p a n -> p (a n)"), ACT.Square,
                                 accum_out=ss2[:, :]).then_inc(s_5z, 1)
                    a.wait_ge(s_5z, t + 1)
                    a.activation(rt2[:, :], ss2[:, :], ACT.Sqrt, scale=1.0 / D, bias=epsc[:, :]).then_inc(s_5rt, 1)
                squares(0)
                squares(1)
                second(0)
                with a.Fori(1, NL - 1) as t:
                    squares(t + 1)
                    evac(t - 1)
                    second(t)
                evac(NL - 2)
                second(NL - 1)
                evac(NL - 1)

            @block.gpsimd
            def _(g):
                def add(t, u):
                    g.wait_ge(s_xr[u], t * 8 + (16 - 8 * u))
                    g.wait_ge(s_5x, t + 1)
                    g.sem_inc(s_tk5, 1)
                    x_ = x1[:, at(t, 1), :].rearrange("p a n -> p (a n)")
                    g.tensor_tensor(x_, x_, xr[u][:, :], ALU.add).then_inc(s_5a, 1)
                    g.wait_ge(s_5a, t + 1)
                    g.dma_start(x1_dram[at(t * P, P), :], x_).then_inc(s_x1s, 16)
                steps(g, 0, NL, add)
                g.wait_ge(s_x1s, 16 * NL)

            @block.vector
            def _(v):
                for k in range(KT):
                    dg = v.tensor_scalar(osq[:, k, :], ident[:, :], mods[:, 2 * KT + k, 0:1], None, ALU.mult)
                dg.then_inc(s_dg, 1)
                v.wait_ge(s_gbm, 1)
                v.tensor_copy(gbc[:, :], PS[:, 6:8, :].rearrange("p a n -> p (a n)")).then_inc(s_gbc, 1)
                v.wait_ge(s_gbc, 1)

                def first(t):
                    v.wait_ge(s_5q, t + 1)
                    v.tensor_reduce(oss[:, :], osq[:, :, :], AX_X, ALU.add).then_inc(s_5s, 1)
                    v.wait_ge(s_5r, t + 1)
                    v.reciprocal(ors[:, :], ort[:, :]).then_inc(s_5i, 1)
                    v.wait_ge(s_5i, t + 1)
                    for g_, o in enumerate((og, og2)):
                        y = v.tensor_tensor(ysb[:, g_ * H:(g_ + 1) * H, :], heads(o[:, at(t, 1), :].rearrange("p a n -> p (a n)")),
                                            bc(ors[:, g_ * H:(g_ + 1) * H], P), ALU.mult)
                    y.then_inc(s_5y, 1)

                def gated(t):
                    v.wait_ge(s_5t, t + 1)
                    for g_, nrm in enumerate((NGDN, NGLA)):
                        e = v.scalar_tensor_tensor(out=yT[:, g_ * H:(g_ + 1) * H, :], in0=heads(PS[:, g_, :]),
                                                   scalar=vcol[:, nrm:nrm + 1], in1=sz[:, g_ * H:(g_ + 1) * H, at(t * P, P)],
                                                   op0=ALU.mult, op1=ALU.mult)
                    e.then_inc(s_5e, 1)

                def residual(t):
                    v.wait_ge(s_5w, t + 1)
                    v.tensor_tensor(x1[:, at(t, 1), :].rearrange("p a n -> p (a n)"),
                                    PS[:, 2:4, :].rearrange("p a n -> p (a n)"), gbc[:, :], ALU.mult).then_inc(s_5x, 1)

                def evac(t):
                    v.wait_ge(s_5u, t + 1)
                    for k in range(4, KT):
                        ev = v.tensor_scalar(h2T[:, k, at(t * P, P)], PS[:, 5, (k - 4) * P:(k - 3) * P],
                                             gain[:, 2 * KT + k:2 * KT + k + 1], mods[:, 3 * KT + k, 0:1], ALU.mult, ALU.add)
                    ev.then_inc(s_5vv, 1)

                def second(t):
                    v.wait_ge(s_5rt, t + 1)
                    v.reciprocal(rs2[:, :], rt2[:, :]).then_inc(s_5ri, 1)
                    v.wait_ge(s_5ri, t + 1)
                    v.tensor_scalar(xn2[:, :], x1[:, at(t, 1), :].rearrange("p a n -> p (a n)"), rs2[:, 0:1], None,
                                    ALU.mult).then_inc(s_5n, 1)
                first(0)
                gated(0)
                first(1)
                residual(0)
                gated(1)
                second(0)
                with v.Fori(1, NL - 1) as t:
                    first(t + 1)
                    residual(t)
                    gated(t + 1)
                    evac(t - 1)
                    second(t)
                residual(NL - 1)
                evac(NL - 2)
                second(NL - 1)
                evac(NL - 1)

        if stop == 5:
            return

        act = place("act", [P, FT, LAT], 95)
        SPLIT = FT - 4
        wu = [[place(f"wu{k}{i}", [P, KT, P], 15 + 8 * k + 4 * i) for i in range(2)] for k in range(2)]
        wlo = [[place(f"wlo{k}{i}", [P, KT, P], 15 + 8 * k + 4 * i, F32R) for i in range(2)] for k in range(2)]
        whi = [[place(f"whi{k}{i}", [P, KT, P], 31 + 8 * k + 4 * i, F32R) for i in range(2)] for k in range(2)]
        h2lo = place("h2lo", [P, KT, LAT], 63, F32R)
        HI_AT = [47 + 4 * k for k in range(4)] + [95 + 4 * (SPLIT + k) for k in range(4)]
        h2hi = [place(f"h2hi{k}", [P, LAT], HI_AT[k], F32R) for k in range(KT)]
        PR, PC = ROWS + 2, GRID + 2
        pad = [place(f"pad{k}", [P, PR, PC], 183 + 4.6875 * k) for k in range(2)]
        acc = [place(f"acc{i}", [P, LAT], 193 + 4 * i) for i in range(2)]

        s_6p = sem("grid_pads_zero")
        s_6w = [[sem(f"w_up_in{k}{i}") for i in range(2)] for k in range(2)]
        s_6m, s_6e, s_6c, s_6v = two("up_product"), two("up_copied"), two("up_centre_tap"), two("up_taps")
        s_6t = two("up_tap_step")
        s_6s, s_6g = sem("up_silu"), sem("gated_product")
        vtap = place("vtap", [P, LAT], 201)
        s_6d, s_6q = sem("up_taps_of_v_but_one"), sem("up_last_tap_of_v")
        s_hh, s_hl, s_hw = sem("h2_high_parts"), sem("h2_low_parts"), sem("h2_whole_again")
        s_wh, s_wl = [sem(f"w_up_high{k}") for k in range(2)], [sem(f"w_up_low{k}") for k in range(2)]

        wd = [place(f"wd{i}", [P, FT, P], 31 + 11 * i) for i in range(2)]
        s_7w = [sem(f"w_down_in{i}") for i in range(2)]
        wdv = w_down[0].rearrange("(f p) n -> p f n", p=P)
        EARLY = FT - 2

        def down_part(pe, u, lo, hi):
            for half in range(2):
                for f in range(lo, hi):
                    mm = pe.matmul(PS[:, 2 * u + half, :], wd[u][:, f, :], act[:, f, half * 512:(half + 1) * 512],
                                   start=(f == 0), stop=(f == FT - 1))
            return mm

        wupv = w_up[0].rearrange("(k p) n -> p k n", p=P)

        with nc.Block() as block:
            @block.sync
            def _(sp):
                def load(f, u, first=False):
                    for k in range(2):
                        if not first:
                            sp.wait_ge(s_6m[k], f - 1)
                        sp.dma_start(wu[k][u][:, :, :], wupv[:, :, at(f * P + k * FF, P)]).then_inc(s_6w[k][u], 16)
                load(0, 0, True)
                load(1, 1, True)
                steps(sp, 2, FT - 2, load)
                sp.wait_ge(s_hw, 1)
                for j in range(2):
                    sp.dma_start(wd[j][:, :, :], wdv[:, :, j * P:(j + 1) * P]).then_inc(s_7w[j], 16)

            @block.tensor
            def _(pe):
                def split_tile(f, u, first=False):
                    for k in range(2):
                        b = 4 * u + 2 * k
                        pe.wait_ge(s_wl[k], f + 1)
                        pe.wait_ge(s_6c[k], f + 1)
                        for half in range(2):
                            cols = slice(half * 512, (half + 1) * 512)
                            for kk in range(KT):
                                if first and k == 0 and half == 0:
                                    pe.wait_ge(s_hl, kk + 1)
                                pe.matmul(PS[:, b + half, :], whi[k][u][:, kk, :], h2hi[kk][:, cols], start=(kk == 0), stop=False)
                                pe.matmul(PS[:, b + half, :], whi[k][u][:, kk, :], h2lo[:, kk, cols], start=False, stop=False)
                                mm = pe.matmul(PS[:, b + half, :], wlo[k][u][:, kk, :], h2hi[kk][:, cols],
                                               start=False, stop=(kk == KT - 1))
                        mm.then_inc(s_6m[k], 1)

                def tile(f, u):
                    for k in range(2):
                        b = 4 * u + 2 * k
                        pe.wait_ge(s_6w[k][u], f * 8 + (16 - 8 * u))
                        pe.wait_ge(s_6c[k], f + 1)
                        for half in range(2):
                            for kk in range(KT):
                                mm = pe.matmul(PS[:, b + half, :], wu[k][u][:, kk, :], h2T[:, kk, half * 512:(half + 1) * 512],
                                               start=(kk == 0), stop=(kk == KT - 1))
                        mm.then_inc(s_6m[k], 1)
                split_tile(0, 0, True)
                split_tile(1, 1)
                steps(pe, 2, SPLIT - 2, split_tile)
                pe.wait_ge(s_hw, 1)
                steps(pe, SPLIT, FT - SPLIT, tile)
                pe.wait_ge(s_7w[0], 16)
                pe.wait_ge(s_6c[0], FT - 1 + 2)
                pe.wait_ge(s_6g, EARLY + 2)
                down_part(pe, 0, 0, EARLY)

            def grid(ap):
                return ap.rearrange("p (r c) -> p r c", c=GRID)

            TAPS = [j for j in range(9) if j != 4]

            def target(k, f, u):
                return acc[u][:, :] if k == 0 else act[:, at(f, 1), :].rearrange("p a n -> p (a n)")

            @block.scalar
            def _(a):
                for k in range(2):
                    a.sem_inc(s_6c[k], 2)
                    a.sem_inc(s_6v[k], 1)
                a.sem_inc(s_6g, 2)

                def high(f, u):
                    for k in range(2):
                        a.wait_ge(s_6w[k][u], f * 8 + (16 - 8 * u))
                        a.activation(whi[k][u][:, :, :], wu[k][u][:, :, :], ACT.Copy).then_inc(s_wh[k], 1)
                high(0, 0)
                for k in range(KT):
                    a.activation(h2hi[k][:, :], h2T[:, k, :], ACT.Copy).then_inc(s_hh, 1)
                high(1, 1)
                a.wait_ge(s_6p, 1)

                def tile(f, u, split):
                    for k in range(2):
                        b = 4 * u + 2 * k
                        src = PS[:, b:b + 2, :].rearrange("p a n -> p (a n)")
                        a.wait_ge(s_6m[k], f + 1)
                        a.wait_ge(s_6v[k], f + 1)
                        a.activation(pad[k][:, 1:PR - 1, 1:PC - 1], grid(src), ACT.Copy).then_inc(s_6e[k], 1)
                        if k == 0:
                            a.wait_ge(s_6g, f + 1)
                        a.activation(target(k, f, u), src, ACT.Identity, scale=fcol[:, at(f + (4 * 2 * FT + k * FT), 1)],
                                     bias=fcol[:, at(f + (9 * 2 * FT + k * FT), 1)]).then_inc(s_6c[k], 1)
                    a.wait_ge(s_6e[1], f + 1)
                    a.activation(grid(vtap[:, :]), pad[1][:, 2:2 + ROWS, 2:2 + GRID], ACT.Copy,
                                 scale=fcol[:, at(f + (TAPS[7] * 2 * FT + FT), 1)]).then_inc(s_6q, 1)
                    if split:
                        high(f + 2, u)
                    a.wait_ge(s_6v[0], f + 2)
                    a.activation(acc[u][:, :], acc[u][:, :], ACT.Silu).then_inc(s_6s, 1)
                steps(a, 0, SPLIT - 2, lambda f, u: tile(f, u, True))
                steps(a, SPLIT - 2, FT - SPLIT + 2, lambda f, u: tile(f, u, False))

            @block.gpsimd
            def _(g):
                def low(f, u):
                    for k in range(2):
                        g.wait_ge(s_wh[k], f + 1)
                        g.tensor_tensor(wlo[k][u][:, :, :], wu[k][u][:, :, :], whi[k][u][:, :, :], ALU.subtract).then_inc(s_wl[k], 1)
                low(0, 0)
                low(1, 1)

                def tile(f, u, split):
                    if split:
                        low(f + 2, u)
                    g.wait_ge(s_6q, f + 1)
                    g.wait_ge(s_6d, f + 1)
                    g.sem_inc(s_tk6, 1)
                    t_ = target(1, f, u)
                    g.tensor_tensor(t_, t_, vtap[:, :], ALU.add).then_inc(s_6v[1], 1)
                    g.wait_ge(s_6s, f + 1)
                    g.wait_ge(s_6v[1], f + 2)
                    g.sem_inc(s_tk6, 1)
                    g.tensor_tensor(t_, t_, acc[u][:, :], ALU.mult).then_inc(s_6g, 1)
                steps(g, 0, SPLIT - 2, lambda f, u: tile(f, u, True))
                steps(g, SPLIT - 2, FT - SPLIT + 2, lambda f, u: tile(f, u, False))

            @block.vector
            def _(v):
                for k in range(KT):
                    v.wait_ge(s_hh, k + 1)
                    v.tensor_tensor(h2lo[:, k, :], h2T[:, k, :], h2hi[k][:, :], ALU.subtract).then_inc(s_hl, 1)
                v.memset(pad[0][:, :, :], 0.0)
                v.memset(pad[1][:, :, :], 0.0).then_inc(s_6p, 1)
                def whole():
                    v.wait_ge(s_6m[1], SPLIT)
                    for k in range(KT):
                        w = v.tensor_tensor(h2T[:, k, :], h2lo[:, k, :], h2hi[k][:, :], ALU.add)
                    w.then_inc(s_hw, 1)

                def tile(f, u, last_split=False):
                    for k in range(2):
                        if k and last_split:
                            whole()
                        v.wait_ge(s_6e[k], f + 1)
                        v.wait_ge(s_6c[k], f + 3)
                        t_ = grid(target(k, f, u))
                        taps = TAPS[:8 - k]
                        last = len(taps) - 1
                        for n, j in enumerate(taps):
                            for hr in range(2):
                                if n:
                                    v.wait_ge(s_6t[k], f * (2 * last) + (2 * n - 1 + hr))
                                r = j // 3 + hr * (ROWS // 2)
                                rows = t_[:, hr * (ROWS // 2):(hr + 1) * (ROWS // 2), :]
                                tp = v.scalar_tensor_tensor(out=rows, in0=pad[k][:, r:r + ROWS // 2, j % 3:j % 3 + GRID],
                                                            scalar=fcol[:, at(f + (j * 2 * FT + k * FT), 1)], in1=rows,
                                                            op0=ALU.mult, op1=ALU.add)
                                if n < last:
                                    tp.then_inc(s_6t[k], 1)
                        tp.then_inc(s_6v[0] if k == 0 else s_6d, 1)
                steps(v, 0, SPLIT - 2, tile)
                tile(SPLIT - 2, 0)
                tile(SPLIT - 1, 1, True)
                steps(v, SPLIT, FT - SPLIT, tile)

        if stop == 6:
            return

        x1b = place("x1b", [P, NL, D], 63)
        yg = [place(f"yg{i}", [P, LAT], 15 + 4 * i) for i in range(2)]
        fsq = place("fsq", [P, NL, D], 31)
        fng = place("fng", [P, D], 23)
        fss = place("fss", [P, NL], 205)
        frt = place("frt", [P, NL], 205.125)
        frs = place("frs", [P, NL], 205.25)

        s_7f = sem("final_gain_in")
        s_7x = sem("x1_again_in")
        s_7m, s_7g, s_7t, s_7a = sem("down_product"), sem("down_gated"), sem("down_turned"), sem("down_added")
        s_7s, s_7r, s_7i, s_7o = sem("final_squares"), sem("final_roots"), sem("final_rstd"), sem("final_tile")
        s_out = sem("out_stored")

        with nc.Block() as block:
            @block.sync
            def _(sp):
                def load(j, u):
                    sp.wait_ge(s_7m, j - 1)
                    sp.dma_start(wd[u][:, :, :], wdv[:, :, at(j * P, P)]).then_inc(s_7w[u], 16)
                sp.dma_start(x1b[:, :, :], x1_dram.rearrange("(t p) n -> p t n", p=P)).then_inc(s_7x, 16)
                sp.dma_start(fng[:, :], final_norm.rearrange("(o n) -> o n", o=1).to_broadcast([P, D])).then_inc(s_7f, 16)
                steps(sp, 2, KT - 2, load)

                def store(t, u):
                    sp.wait_ge(s_7o, t + 1)
                    sp.dma_start(out[0][at(t * P, P), :], x1b[:, at(t, 1), :].rearrange("p a n -> p (a n)")).then_inc(s_out, 16)
                steps(sp, 0, NL, store)
                sp.wait_ge(s_out, 16 * NL)

            @block.tensor
            def _(pe):
                def down(i, u, lo=0):
                    pe.wait_ge(s_7w[u], i * 16 + 16)
                    down_part(pe, u, lo, FT).then_inc(s_7m, 1)

                def turn(i, u):
                    pe.wait_ge(s_7g, i * 2 + (u + 1))
                    pe.wait_ge(s_7a, i * 2 + (u + 1))
                    for t in range(NL):
                        tr = pe.transpose(PS[:, 4 + 2 * u + t // 4, (t % 4) * P:(t % 4 + 1) * P], yg[u][:, t * P:(t + 1) * P], ident[:, :])
                    tr.then_inc(s_7t, 1)
                down(0, 0, EARLY)
                down(0, 1)
                turn(0, 0)
                turn(0, 1)
                with pe.Fori(1, KT // 2) as i:
                    down(i, 0)
                    down(i, 1)
                    turn(i, 0)
                    turn(i, 1)

            @block.scalar
            def _(a):
                def gate(j, u):
                    a.wait_ge(s_7m, j + 1)
                    a.activation(yg[u][:, :], PS[:, 2 * u:2 * u + 2, :].rearrange("p a n -> p (a n)"), ACT.Identity,
                                 scale=mods[:, at(j + 5 * KT, 1), 0:1].rearrange("p a b -> p (a b)"), bias=0.0).then_inc(s_7g, 1)
                steps(a, 0, KT, gate)
                a.wait_ge(s_7a, KT + 2)
                for t in range(NL):
                    sq = a.activation(fsq[:, t, :], x1b[:, t, :], ACT.Square, accum_out=fss[:, t:t + 1])
                sq.then_inc(s_7s, 1)
                a.wait_ge(s_7s, 1)
                a.activation(frt[:, :], fss[:, :], ACT.Sqrt, scale=1.0 / D, bias=epsc[:, :]).then_inc(s_7r, 1)

            @block.vector
            def _(v):
                v.sem_inc(s_7a, 2)
                v.wait_ge(s_7x, 16)

                def add(j, u):
                    v.wait_ge(s_7t, j + 1)
                    x_ = x1b[:, :, at(j * P, P)]
                    v.tensor_tensor(x_, PS[:, 4 + 2 * u:6 + 2 * u, :].rearrange("p a (c n) -> p (a c) n", n=P), x_, ALU.add).then_inc(s_7a, 1)
                steps(v, 0, KT, add)
                v.wait_ge(s_7r, 1)
                v.reciprocal(frs[:, :], frt[:, :]).then_inc(s_7i, 1)
                v.wait_ge(s_7i, 1)
                v.wait_ge(s_7f, 16)

                def finish(t, u):
                    x_ = x1b[:, at(t, 1), :].rearrange("p a n -> p (a n)")
                    v.scalar_tensor_tensor(out=x_, in0=x_, scalar=frs[:, at(t, 1)], in1=fng[:, :],
                                           op0=ALU.mult, op1=ALU.mult).then_inc(s_7o, 1)
                steps(v, 0, NL, finish)


_INS = ["x", "c", "ctx", "c_ctx", "w_mod", "b_mod", "norm1", "w_in", "gdn_conv", "gdn_a_log", "gdn_dt_bias", "gdn_norm",
        "gla_w_gk", "gla_b_gk", "gla_norm", "w_out", "norm2", "w_up", "ffn_conv", "ffn_conv_b", "w_down", "final_norm"]


def kernel(**inputs):
    import numpy as _np
    import concourse.bacc as _bacc
    from concourse import mybir as _mybir
    from concourse.bass_utils import run_bass_kernel_spmd as _run

    nc = _bacc.Bacc("TRN2", target_bir_lowering=False, num_devices=1)
    arrays, args = {}, []
    for name in _INS:
        a = _np.ascontiguousarray(inputs[name])
        arrays[f"in_{name}_dram"] = a
        args.append(nc.dram_tensor(f"in_{name}_dram", a.shape, _mybir.dt.from_np(a.dtype), kind="ExternalInput").ap())
    args.append(nc.dram_tensor("out_0_dram", (1, LAT, D), F32, kind="ExternalOutput").ap())
    program(nc, *args)
    r = _run(nc, [arrays], core_ids=[0])
    return r.results[0]["out_0_dram"]
```
